# Optimizing a Trainium2 kernel written in Bass

```python
import math
import jax, jax.numpy as jnp
from jax import lax
import numpy as np

D_MODEL = 1024
BATCH = 1
SEQ = 512
DEPTH = 1

MIX_WIDTH = D_MODEL
SGU_WIDTH = MIX_WIDTH // 2
SGU_HEADS = 4
SGU_HEAD_DIM = SGU_WIDTH // SGU_HEADS
SGU_CHUNK = 128
RET_WIDTH = MIX_WIDTH - SGU_WIDTH
RET_HEADS = 4
RET_HEAD_DIM = RET_WIDTH // RET_HEADS
RET_CHUNK = 128
ROPE_BASE = 10000.0
IN_WIDTH = 2 * SGU_WIDTH + 4 * RET_WIDTH
IN_SPLITS = (SGU_WIDTH, 2 * SGU_WIDTH, 2 * SGU_WIDTH + RET_WIDTH,
             2 * SGU_WIDTH + 2 * RET_WIDTH, 2 * SGU_WIDTH + 3 * RET_WIDTH)
PEER_HEADS = 8
PEER_N_KEYS = 128
PEER_N_EXPERTS = PEER_N_KEYS * PEER_N_KEYS
PEER_TOPK = 16
PEER_QUERY_DIM = 256
PEER_KEY_DIM = PEER_QUERY_DIM // 2
PEER_TOKEN_BLOCK = 128
LN_EPS = 1e-5
GN_EPS = 1e-5
DEEPNORM_ALPHA = (2.0 * DEPTH) ** 0.25
DEEPNORM_BETA = (8.0 * DEPTH) ** -0.25

kernel_name = "hybrid_sgu_retention_peer_deepnorm"

def _layer_norm(x, w, b):
    xf = x.astype(jnp.float32)
    mu = xf.mean(-1, keepdims=True)
    var = jnp.square(xf - mu).mean(-1, keepdims=True)
    return ((xf - mu) * lax.rsqrt(var + LN_EPS) * w + b).astype(x.dtype)

def _rotary(x):
    s, dh = x.shape[1], x.shape[-1]
    half = dh // 2
    inv = ROPE_BASE ** (-jnp.arange(half, dtype=jnp.float32) / half)
    ang = jnp.arange(s, dtype=jnp.float32)[:, None] * inv[None, :]
    cos = jnp.cos(ang)[:, None, :]
    sin = jnp.sin(ang)[:, None, :]
    x1, x2 = x[..., :half], x[..., half:]
    return jnp.concatenate([x1 * cos - x2 * sin, x1 * sin + x2 * cos], -1).astype(x.dtype)

def _spatial_gating_group(u, v, ln_w, ln_b, w_s, b_s):
    u = jax.nn.gelu(u, approximate=False)
    v = _layer_norm(jax.nn.gelu(v, approximate=False), ln_w, ln_b)
    b, s, w = v.shape
    c = s // SGU_CHUNK
    vr = v.reshape(b, c, SGU_CHUNK, SGU_HEADS, SGU_HEAD_DIM)
    mixed = jnp.einsum('hlm,bcmhd->bclhd', w_s, vr) + b_s.T[None, None, :, :, None]
    return u * mixed.reshape(b, s, w).astype(u.dtype)

def _retention_one_direction(q, k, v, log_g, include_diag):
    b, h, s, dk = q.shape
    dv = v.shape[-1]
    L = RET_CHUNK
    c = s // L
    q = q.reshape(b, h, c, L, dk)
    k = k.reshape(b, h, c, L, dk)
    v = v.reshape(b, h, c, L, dv)
    pos = jnp.arange(L, dtype=jnp.float32)
    diff = pos[:, None] - pos[None, :]
    mask = (diff >= 0) if include_diag else (diff > 0)
    decay = jnp.where(mask[None], jnp.exp(jnp.maximum(diff, 0.0)[None] * log_g[:, None, None]), 0.0)
    scores = jnp.einsum('bhcld,bhcmd->bhclm', q, k) * decay[None, :, None]
    o_inner = jnp.einsum('bhclm,bhcmv->bhclv', scores, v)
    k_w = jnp.exp((L - 1 - pos)[None, :] * log_g[:, None])
    chunk_state = jnp.einsum('bhcld,bhclv->bhcdv', k * k_w[None, :, None, :, None], v)
    g_chunk = jnp.exp(L * log_g)[:, None, None]

    def step(state, s_c):
        return g_chunk * state + s_c, state

    _, prev = lax.scan(step, jnp.zeros_like(chunk_state[:, :, 0]), jnp.moveaxis(chunk_state, 2, 0))
    prev = jnp.moveaxis(prev, 0, 2)
    q_w = jnp.exp((pos + 1.0)[None, :] * log_g[:, None])
    o_cross = jnp.einsum('bhcld,bhcdv->bhclv', q * q_w[None, :, None, :, None], prev)
    return (o_inner + o_cross).reshape(b, h, s, dv)

def _retention_group(q, k, v, g, decay_fwd, decay_bwd, gn_w):
    b, s, _ = q.shape
    out_dtype = q.dtype
    q = _rotary(q.reshape(b, s, RET_HEADS, RET_HEAD_DIM))
    k = _rotary(k.reshape(b, s, RET_HEADS, RET_HEAD_DIM)) * (RET_HEAD_DIM ** -0.5)
    v = v.reshape(b, s, RET_HEADS, RET_HEAD_DIM)
    q, k, v = (t.transpose(0, 2, 1, 3) for t in (q, k, v))
    lg_f = jax.nn.log_sigmoid(decay_fwd.astype(jnp.float32))
    lg_b = jax.nn.log_sigmoid(decay_bwd.astype(jnp.float32))
    o_f = _retention_one_direction(q, k, v, lg_f, True)
    flip = lambda t: jnp.flip(t, axis=2)
    o_b = flip(_retention_one_direction(flip(q), flip(k), flip(v), lg_b, False))
    o = (o_f + o_b).transpose(0, 2, 1, 3).astype(jnp.float32)
    mu = o.mean(-1, keepdims=True)
    var = jnp.square(o - mu).mean(-1, keepdims=True)
    on = ((o - mu) * lax.rsqrt(var + GN_EPS)).reshape(b, s, RET_WIDTH) * gn_w
    return (jax.nn.silu(g.astype(jnp.float32)) * on).astype(out_dtype)

def _peer(h, w_q, sub_keys, u_tab, v_tab):
    b, s, d = h.shape
    q = (h @ w_q).reshape(b, s, PEER_HEADS, 2, PEER_KEY_DIM)
    scores = jnp.einsum('bshpd,hpnd->bshpn', q, sub_keys)
    top_s, top_i = lax.top_k(scores, PEER_TOPK)
    cand_s = top_s[..., 0, :, None] + top_s[..., 1, None, :]
    cand_i = top_i[..., 0, :, None] * PEER_N_KEYS + top_i[..., 1, None, :]
    cand_s = cand_s.reshape(b, s, PEER_HEADS, PEER_TOPK * PEER_TOPK)
    cand_i = cand_i.reshape(b, s, PEER_HEADS, PEER_TOPK * PEER_TOPK)
    best_s, best_pos = lax.top_k(cand_s, PEER_TOPK)
    expert_idx = jnp.take_along_axis(cand_i, best_pos, axis=-1)
    gates = jax.nn.softmax(best_s.astype(jnp.float32), axis=-1)
    n_blocks = (b * s) // PEER_TOKEN_BLOCK
    n_sel = PEER_HEADS * PEER_TOPK
    xb = h.reshape(n_blocks, PEER_TOKEN_BLOCK, d)
    ib = expert_idx.reshape(n_blocks, PEER_TOKEN_BLOCK, n_sel)
    gb = gates.reshape(n_blocks, PEER_TOKEN_BLOCK, n_sel).astype(h.dtype)

    def block(args):
        xt, it, gt = args
        act = jax.nn.gelu(jnp.einsum('td,ted->te', xt, u_tab[it]), approximate=False)
        return jnp.einsum('te,ted->td', gt * act, v_tab[it])

    out = lax.map(block, (xb, ib, gb))
    return out.reshape(b, s, d)

def setup_inputs(seed: int = 0) -> dict:
    key = jax.random.key(seed)
    ks = jax.random.split(key, 20)
    f32 = jnp.float32
    nrm = lambda k, shape, scale: jax.random.normal(k, shape, f32) * scale
    base_decay = jnp.asarray(np.log(2.0 ** (5.0 + np.arange(RET_HEADS)) - 1.0), f32)
    return {
        "x": jax.random.normal(ks[0], (BATCH, SEQ, D_MODEL), f32),
        "w_in": nrm(ks[1], (DEPTH, D_MODEL, IN_WIDTH), D_MODEL ** -0.5),
        "sgu_ln_w": 1.0 + nrm(ks[2], (DEPTH, SGU_WIDTH), 0.02),
        "sgu_ln_b": nrm(ks[3], (DEPTH, SGU_WIDTH), 0.02),
        "sgu_w_s": nrm(ks[4], (DEPTH, SGU_HEADS, SGU_CHUNK, SGU_CHUNK), SGU_CHUNK ** -0.5),
        "sgu_b": 1.0 + nrm(ks[5], (DEPTH, SGU_HEADS, SGU_CHUNK), 0.02),
        "ret_decay_fwd": base_decay[None] + nrm(ks[6], (DEPTH, RET_HEADS), 0.05),
        "ret_decay_bwd": base_decay[None] + nrm(ks[7], (DEPTH, RET_HEADS), 0.05),
        "ret_gn_w": 1.0 + nrm(ks[8], (DEPTH, RET_WIDTH), 0.02),
        "w_out": nrm(ks[9], (DEPTH, MIX_WIDTH, D_MODEL), DEEPNORM_BETA * MIX_WIDTH ** -0.5),
        "ln1_w": 1.0 + nrm(ks[10], (DEPTH, D_MODEL), 0.02),
        "ln1_b": nrm(ks[11], (DEPTH, D_MODEL), 0.02),
        "peer_w_q": nrm(ks[12], (DEPTH, D_MODEL, PEER_HEADS * PEER_QUERY_DIM), D_MODEL ** -0.5),
        "peer_sub_keys": nrm(ks[13], (DEPTH, PEER_HEADS, 2, PEER_N_KEYS, PEER_KEY_DIM), PEER_KEY_DIM ** -0.5),
        "peer_u": nrm(ks[14], (DEPTH, PEER_N_EXPERTS, D_MODEL), D_MODEL ** -0.5),
        "peer_v": nrm(ks[15], (DEPTH, PEER_N_EXPERTS, D_MODEL), DEEPNORM_BETA),
        "ln2_w": 1.0 + nrm(ks[16], (DEPTH, D_MODEL), 0.02),
        "ln2_b": nrm(ks[17], (DEPTH, D_MODEL), 0.02),
    }

def reference(x, w_in, sgu_ln_w, sgu_ln_b, sgu_w_s, sgu_b, ret_decay_fwd, ret_decay_bwd, ret_gn_w,
              w_out, ln1_w, ln1_b, peer_w_q, peer_sub_keys, peer_u, peer_v, ln2_w, ln2_b):
    for l in range(DEPTH):
        proj = x @ w_in[l]
        a_u, a_v, r_q, r_k, r_v, r_g = jnp.split(proj, IN_SPLITS, axis=-1)
        a_out = _spatial_gating_group(a_u, a_v, sgu_ln_w[l], sgu_ln_b[l], sgu_w_s[l], sgu_b[l])
        r_out = _retention_group(r_q, r_k, r_v, r_g, ret_decay_fwd[l], ret_decay_bwd[l], ret_gn_w[l])
        mixed = jnp.concatenate([a_out, r_out], axis=-1) @ w_out[l]
        h = _layer_norm(DEEPNORM_ALPHA * x + mixed, ln1_w[l], ln1_b[l])
        ffn = _peer(h, peer_w_q[l], peer_sub_keys[l], peer_u[l], peer_v[l])
        x = _layer_norm(DEEPNORM_ALPHA * h + ffn, ln2_w[l], ln2_b[l])
    return x


_drawn_inputs = setup_inputs


def setup_inputs(seed=0):
    import zlib

    import numpy as np

    out = dict(_drawn_inputs(seed))
    spreads = {}
    factors = {'sgu_ln_w': 3.209,
     'sgu_ln_b': 3.275,
     'sgu_b': 3.139,
     'ret_gn_w': 3.358,
     'ln2_w': 2.855,
     'ln2_b': 2.874}
    for name, (base, spread) in spreads.items():
        noise = np.random.default_rng([zlib.crc32(name.encode()), seed]).standard_normal(out[name].shape)
        drawn = base * np.exp(spread * noise) if base else spread * noise
        out[name] = __import__('jax').numpy.asarray(drawn.astype(out[name].dtype))
    for name, factor in factors.items():
        out[name] = (out[name] * factor).astype(out[name].dtype)
    return out
```

```python
import numpy as np
import concourse.bass as bass
from concourse import mybir
from contextlib import ExitStack

P = 128
SEQ, D = 512, 1024
NT = SEQ // P
KC = D // P
GW = 512
HEADS = 4
PH, TOPK, NK = 8, 16, 128
UNITS = NT * PH
RING = 8
NDIAG = 8
ALPHA = 2.0 ** 0.25
EPS = 1e-5
SCALE = float(P) ** -0.5
STRIP = 2 * SEQ - P
NEG = -3.0e38
GV, GU, GQ, GK, GRV, GG, GO0, GO1 = range(8)
GROUP_COL = {GV: 512, GU: 0, GQ: 1024, GK: 1536, GRV: 2048, GG: 2560, GO0: 0, GO1: 512}
WRING = 4


def phase_a_jobs():
    jobs = []

    def add(kind, *arg, by):
        jobs.append((kind, arg, by))

    for t in range(NT):
        add("xT", t, 0, by="act")
        add("xT", t, 1, by="dve")
    for t in range(NT):
        add("gv", t, by="act")
    add("wsT", by="act")
    for q in range(4):
        add("keysT", q, by="dve")
    for c in range(4):
        add("gu", c, by="act")
    for h in range(HEADS):
        add("mix", h, by="dve")
    for w, kind in ((0, "rot"), (1, "rot")):
        for t in range(NT):
            add("qk", w, t, by="dve")
            if t:
                add("qkT", w, t - 1, by="act")
        add("qkT", w, NT - 1, by="act")
    for t in range(NT):
        add("rv", t, by="act")
    for t in range(NT):
        add("rg", t, by="act")
    for h in range(HEADS):
        for m in range(NT):
            add("score", h, m, by="dve")
        if h >= 1:
            add("read", h - 1, by="dve")
        if h >= 2:
            add("rT", h - 2, by="act")
    add("read", HEADS - 1, by="dve")
    add("rT", HEADS - 2, by="act")
    add("rT", HEADS - 1, by="act")
    for t in range(NT):
        add("out", t, 0, by="dve")
        add("out", t, 1, by="dve")
        if t:
            add("hT", t - 1, 0, by="act")
            add("hT", t - 1, 1, by="act")
    add("hT", NT - 1, 0, by="act")
    add("hT", NT - 1, 1, by="act")
    placed, used = [], [0] * 8
    for i, (kind, arg, by) in enumerate(jobs):
        b = i % 8
        placed.append((kind, arg, by, b, used[b]))
        used[b] += 1
    return placed, used


def head_jobs(used):
    out, used = [], list(used)
    for h in range(PH):
        this = []
        for kind, first in (("query", 4), ("keys", 6)):
            for p in range(2):
                this.append((kind, (h, p), "act", first + p, used[first + p]))
                used[first + p] += 1
        out.append(this)
    return out


def layer(nc, x, w_in, sgu_ln_w, sgu_ln_b, sgu_w_s, sgu_b, decay_fwd, decay_bwd, gn_w, w_out, ln1_w, ln1_b,
          w_q, sub_keys, peer_u, peer_v, ln2_w, ln2_b, rope, out):
    f32, i32 = mybir.dt.float32, mybir.dt.int32
    u32 = mybir.dt.uint32
    ALU, ACT = mybir.AluOpType, mybir.ActivationFunctionType
    AX = mybir.AxisListType

    JOBS, USED = phase_a_jobs()
    HJOBS = head_jobs(USED)

    ctx = ExitStack()
    with ctx:
        def sb(name, shape, dt=f32):
            return ctx.enter_context(nc.sbuf_tensor(name, shape, dt))

        def sem(name):
            return ctx.enter_context(nc.semaphore(name))

        big = sb("big", [P, 2 * RING * D])
        wring = big[:, :].rearrange("p (s k n) -> p s k n", s=WRING, k=KC)
        rows = big[:, :].rearrange("p (s n) -> p s n", n=D)
        urow = [rows[:, s, :] for s in range(RING)]
        vrow = [rows[:, RING + s, :] for s in range(RING)]
        xh = sb("xh", [P, NT * D])
        xT = sb("xT", [P, KC, SEQ])
        prob1 = xT[:, 0:4, :]
        rnorm = xT[:, 4:8, :]
        y = sb("y", [P, NT * D])
        strip = y[:, 0:HEADS * STRIP].rearrange("p (h n) -> p h n", h=HEADS)
        S = sb("S", [P, UNITS * 256 + 512])
        S4 = S[:, 0:UNITS * 256].rearrange("p (t q n) -> p t q n", t=NT, q=2 * PH)
        rv = S[:, 0:2048].rearrange("p (t n) -> p t n", t=NT)
        gate = S[:, 2048:4096].rearrange("p (t n) -> p t n", t=NT)
        keys_raw = S[:, 2048:4096].rearrange("p (q n) -> p q n", q=2 * PH)
        gains = S[:, 4096:6144].rearrange("p (g n) -> p g n", g=4)
        prob0 = S[:, 6144:8192].rearrange("p (m n) -> p m n", m=NT)
        ws_raw = S[:, 6144:6656].rearrange("p (h n) -> p h n", h=HEADS)
        tmp = S[:, 6144:8192].rearrange("p (m n) -> p m n", m=NT)
        prob = [prob0, prob1]
        mixT = sb("mixT", [P, KC, SEQ])
        vln = mixT[:, 4:8, :]
        mix1 = mixT[:, :, :].rearrange("p k n -> p (k n)")
        hcur = mix1[:, 0:D]
        qh = mix1[:, D:D + 2 * 1024].rearrange("p (s q n) -> p s q n", s=2, q=2)
        eq = mix1[:, 3 * D:3 * D + 512]
        sc = mix1[:, 3 * D + 512:4 * D].rearrange("p (a n) -> p a n", a=2)
        qkT = sb("qkT", [P, 2, HEADS, SEQ])
        qk1 = qkT[:, :, :, :].rearrange("p a h n -> p (a h n)")
        ahead, behind, part = (qk1[:, 1024 * i:1024 * i + STRIP] for i in range(3))
        wq = qk1.rearrange("p (s k n) -> p s k n", s=2, k=KC)
        lnp = sb("lnp", [P, 2, D])
        keysT = sb("keysT", [P, 2 * PH, NK])
        wsT = sb("wsT", [P, HEADS, P])
        ropet = sb("ropet", [P, NT, 2, 64])
        ident = sb("ident", [P, P])
        diag = sb("diag", [P, NDIAG, P])
        iota16 = sb("iota16", [P, TOPK])
        dec = sb("dec", [P, 10, 2 * HEADS])
        st = sb("st", [P, 4, 6])
        mv = sb("mv", [P, 4, 2])
        nw = sb("nw", [P, 4, 4])
        cand = sb("cand", [P, 256])
        top = sb("top", [P, 2, TOPK])
        topi = sb("topi", [P, 2, TOPK], u32)
        topf = sb("topf", [P, 2, TOPK])
        best = sb("best", [P, 2, TOPK])
        pos = sb("pos", [P, TOPK], u32)
        posab = sb("posab", [P, 2, TOPK], u32)
        posf = sb("posf", [P, 2, TOPK])
        pick = sb("pick", [P, 2, TOPK])
        eid = sb("eid", [P, 2, TOPK], i32)
        idx = sb("idx", [P, 2, TOPK], i32)
        negmax = sb("negmax", [P, 2])
        esum = sb("esum", [P, 2])
        rsum = sb("rsum", [P, 2])
        eg = sb("eg", [P, 2, TOPK])
        dots = sb("dots", [P, 2, TOPK])
        gel = sb("gel", [P, 2, TOPK])
        wgt = sb("wgt", [P, 2, TOPK])
        ps = ctx.enter_context(nc.psum_tensor("ps", [P, 8, 512], f32))
        acc = [ps[:, 2 * k:2 * k + 2, :].rearrange("p a n -> p (a n)") for k in range(2)]

        full = [sem(f"bank_full{b}") for b in range(8)]
        free = [sem(f"bank_free{b}") for b in range(8)]
        s_x = [sem(f"x_loaded{t}") for t in range(NT)]
        s_w = [sem(f"weights_loaded{s}") for s in range(WRING)]
        s_wdone = sem("weights_used")
        s_ws, s_keys, s_rope = sem("ws_loaded"), sem("keys_loaded"), sem("rope_loaded")
        s_gain, s_dec, s_ln = sem("gains_loaded"), sem("decay_loaded"), sem("ln_loaded")
        s_const = sem("constants_ready")
        s_xT = sem("xT_ready")
        s_wsT, s_keysT = sem("wsT_ready"), sem("keysT_ready")
        s_gv, s_vln = sem("gelu_v_ready"), sem("vln_ready")
        s_gu, s_mix = sem("gelu_u_ready"), sem("gating_ready")
        s_adec, s_edec, s_z, s_strip = sem("absdecay_ready"), sem("expdecay_ready"), sem("logstrip_ready"), sem("strip_ready")
        s_rot, s_qkT = sem("rotated_ready"), sem("qkT_ready")
        s_rv, s_gate = sem("rv_ready"), sem("gate_ready")
        s_scored = sem("scores_done")
        s_prob, s_rn, s_rT = sem("prob_ready"), sem("retention_ready"), sem("retentionT_ready")
        s_h, s_hT, s_y = sem("h_ready"), sem("hT_ready"), sem("y_started")
        s_wq = [sem(f"wq_loaded{s}") for s in range(2)]
        s_wqd = sem("wq_used")
        s_qh, s_sc = sem("query_ready"), sem("key_scores_ready")
        s_best, s_exp = sem("best_ready"), sem("exp_ready")
        s_idx = sem("indices_ready")
        s_u = [sem(f"urow_gathered{s}") for s in range(RING)]
        s_v = [sem(f"vrow_gathered{s}") for s in range(RING)]
        s_dot, s_gel, s_wgt = sem("dots_done"), sem("gelu_ready"), sem("expert_weights_ready")
        s_diag, s_vexp = sem("diag_ready"), sem("experts_added")
        s_yadd = sem("unit_added")
        s_ln2, s_out = sem("output_ready"), sem("output_stored")

        peer_u2, peer_v2 = peer_u[0], peer_v[0]
        w_in3 = w_in[0].rearrange("(k p) n -> p k n", p=P)
        w_out3 = w_out[0].rearrange("(k p) n -> p k n", p=P)
        w_q3 = w_q[0].rearrange("(k p) n -> p k n", p=P)
        out3 = out[0].rearrange("(t p) n -> p t n", p=P)

        block = ctx.enter_context(nc.Block())

        @block.sync
        def _(sp):
            def load_group(g):
                if g >= WRING:
                    sp.wait_ge(s_wdone, g - WRING + 1)
                src = w_out3 if g >= GO0 else w_in3
                c = GROUP_COL[g]
                sp.dma_start(wring[:, g % WRING, :, :], src[:, :, c:c + GW]).then_inc(s_w[g % WRING], 16)

            for t in range(NT):
                sp.dma_start(xh[:, t * D:(t + 1) * D], x[0, t * P:(t + 1) * P, :]).then_inc(s_x[t], 16)
            for g in range(8):
                load_group(g)
            sp.wait_ge(s_scored, 1)
            for h in range(PH):
                if h >= 2:
                    sp.wait_ge(s_wqd, h - 1)
                sp.dma_start(wq[:, h % 2, :, :], w_q3[:, :, h * 256:(h + 1) * 256]).then_inc(s_wq[h % 2], 16)
                if h == 1:
                    sp.wait_ge(s_h, NT)
                    sp.dma_start(lnp[:, 0, :], ln2_w[0].partition_broadcast(P)).then_inc(s_ln, 16)
                    sp.dma_start(lnp[:, 1, :], ln2_b[0].partition_broadcast(P)).then_inc(s_ln, 16)
            for t in range(NT):
                sp.wait_ge(s_ln2, t + 1)
                sp.dma_start(out3[:, t, :], y[:, t * D:(t + 1) * D]).then_inc(s_out, 16)
            sp.wait_ge(s_out, 16 * NT)

        @block.gpsimd
        def _(pool):
            nc.gpsimd.memset(ident[:], 0.0).then_inc(s_const, 1)
            nc.gpsimd.memset(S[:, UNITS * 256:], 0.0).then_inc(s_const, 1)
            nc.gpsimd.iota(iota16[:], pattern=[[1, TOPK]], base=0, channel_multiplier=0,
                           allow_small_or_imprecise_dtypes=True).then_inc(s_const, 1)
            nc.gpsimd.iota(ahead, pattern=[[1, STRIP]], base=-(SEQ - P), channel_multiplier=-1,
                           allow_small_or_imprecise_dtypes=True).then_inc(s_const, 1)
            pool.wait_ge(s_const, 1)
            nc.gpsimd.affine_select(out=ident[:], in_=ident[:], compare_op=ALU.not_equal, fill=1.0, base=0,
                                    pattern=[[-1, P]], channel_multiplier=1).then_inc(s_const, 1)
            pool.wait_ge(s_wdone, 8)

            def gathers(u, k, first):
                pool.wait_ge(s_idx, u + 1)
                pool.nop(nofuse=True)
                for e in range(TOPK):
                    if e % 4 == 0 and not (first and e < RING):
                        pool.wait_ge(s_dot, 16 * u + e + 4 - RING)
                        pool.nop(nofuse=True)
                    nc.gpsimd.indirect_dma_start(
                        urow[e % RING], None, peer_u2,
                        bass.IndirectOffsetOnAxis(ap=idx[:, k, e:e + 1], axis=0)).then_inc(s_u[e % RING], 16)
                for e in range(TOPK):
                    if e % 4 == 0 and not (first and e < RING):
                        pool.wait_ge(s_vexp, 16 * u + e + 4 - RING)
                        pool.nop(nofuse=True)
                    nc.gpsimd.indirect_dma_start(
                        vrow[e % RING], None, peer_v2,
                        bass.IndirectOffsetOnAxis(ap=idx[:, k, e:e + 1], axis=0)).then_inc(s_v[e % RING], 16)

            gathers(0, 0, True)
            gathers(1, 1, False)
            with pool.Fori(1, UNITS // 2) as pair:
                gathers(2 * pair, 0, False)
                gathers(2 * pair + 1, 1, False)

        @block.scalar
        def _(act):
            A = nc.scalar

            def copy(dst, src):
                return A.activation(dst, src, ACT.Copy)

            act.dma_start(dec[:, 0, 0:HEADS], decay_fwd[0].partition_broadcast(P)).then_inc(s_dec, 16)
            act.dma_start(dec[:, 0, HEADS:], decay_bwd[0].partition_broadcast(P)).then_inc(s_dec, 16)
            act.dma_start(gains[:, 0, :], sgu_ln_w[0].partition_broadcast(P)).then_inc(s_gain, 16)
            act.dma_start(gains[:, 1, :], sgu_ln_b[0].partition_broadcast(P)).then_inc(s_gain, 16)
            act.dma_start(gains[:, 2, :], gn_w[0].partition_broadcast(P)).then_inc(s_gain, 16)
            act.dma_start(gains[:, 3, :], sgu_b[0].rearrange("h l -> (h l)").partition_broadcast(P)).then_inc(s_gain, 16)
            act.dma_start(ws_raw, sgu_w_s[0].rearrange("h l m -> l h m")).then_inc(s_ws, 16)
            act.dma_start(keys_raw, sub_keys[0].rearrange("h q n d -> n (h q) d")).then_inc(s_keys, 16)
            act.dma_start(ropet[:], rope).then_inc(s_rope, 16)
            act.dma_start(lnp[:, 0, :], ln1_w[0].partition_broadcast(P)).then_inc(s_ln, 16)
            act.dma_start(lnp[:, 1, :], ln1_b[0].partition_broadcast(P)).then_inc(s_ln, 16)

            act.wait_ge(s_adec, 1)
            A.activation(dec[:, 3, :], dec[:, 2, :], ACT.Exp, scale=-1.0).then_inc(s_edec, 1)
            done_h = 0
            for kind, arg, by, b, n in JOBS:
                if by != "act":
                    continue
                act.wait_ge(full[b], n + 1)
                bank = ps[:, b, :]
                bank4 = bank.rearrange("p (c n) -> p c n", c=4)
                if kind == "xT":
                    t = arg[0]
                    copy(xT[:, 0:4, t * P:(t + 1) * P], bank4).then_inc(free[b], 1)
                    A.drain().then_inc(s_xT, 1)
                elif kind == "gv":
                    A.activation(vln[:, arg[0], :], bank, ACT.Gelu).then_inc(free[b], 1)
                    A.drain().then_inc(s_gv, 1)
                elif kind == "wsT":
                    copy(wsT[:], bank4).then_inc(free[b], 1)
                    A.drain().then_inc(s_wsT, 1)
                elif kind == "gu":
                    A.activation(mixT[:, arg[0], :], bank, ACT.Gelu).then_inc(free[b], 1)
                    A.drain().then_inc(s_gu, 1)
                    if arg[0] == 3:
                        for h in range(HEADS):
                            act.wait_ge(s_z, h + 1)
                            A.activation(strip[:, h, :], strip[:, h, :], ACT.Exp).then_inc(s_strip, 1)
                elif kind == "qkT":
                    w, t = arg
                    copy(qkT[:, w, :, t * P:(t + 1) * P], bank4).then_inc(free[b], 1)
                    A.drain().then_inc(s_qkT, 1)
                elif kind == "rv":
                    copy(rv[:, arg[0], :], bank).then_inc(free[b], 1)
                    A.drain().then_inc(s_rv, 1)
                elif kind == "rg":
                    A.activation(gate[:, arg[0], :], bank, ACT.Silu).then_inc(free[b], 1)
                    A.drain().then_inc(s_gate, 1)
                elif kind == "rT":
                    copy(mixT[:, 4 + arg[0], :], bank).then_inc(free[b], 1)
                    A.drain().then_inc(s_rT, 1)
                elif kind == "hT":
                    t, half = arg
                    copy(xT[:, 4 * half:4 * half + 4, t * P:(t + 1) * P], bank4).then_inc(free[b], 1)
                    A.drain().then_inc(s_hT, 1)
                    if half == 1:
                        A.activation(y[:, t * D:(t + 1) * D], xh[:, t * D:(t + 1) * D], ACT.Copy,
                                     scale=ALPHA).then_inc(s_y, 1)

            def head_copies(h):
                for kind, (_, p), _, b, n in HJOBS[h]:
                    act.wait_ge(full[b], n + 1)
                    if kind == "query":
                        copy(qh[:, h % 2, p, :], ps[:, b, :]).then_inc(free[b], 1)
                        A.drain().then_inc(s_qh, 1)
                    else:
                        copy(S4[:, :, 2 * h + p, :],
                             ps[:, b, :].rearrange("p (c n) -> p c n", c=4)).then_inc(free[b], 1)
                        A.drain().then_inc(s_sc, 1)

            def exps(u, k):
                act.wait_ge(s_best, u + 1)
                A.activation(eg[:, k, :], best[:, k, :], ACT.Exp, bias=negmax[:, k:k + 1],
                             accum_out=esum[:, k:k + 1]).then_inc(s_exp, 1)

            def unit(u, k, first):
                act.wait_ge(s_dot, 16 * u + 16)
                A.activation(gel[:, k, :], dots[:, k, :], ACT.Gelu).then_inc(s_gel, 1)
                act.wait_ge(s_wgt, u + 1)
                for e in range(TOPK):
                    if e % 4 == 0 and not (first and e < NDIAG):
                        act.wait_ge(s_vexp, 16 * u + e + 4 - NDIAG)
                    A.activation(diag[:, e % NDIAG, :], ident[:], ACT.Copy,
                                 scale=wgt[:, k, e:e + 1]).then_inc(s_diag, 1)
                exps(u + 2, k)

            for h in range(4):
                head_copies(h)
                if h < 2:
                    exps(h, h)
            act.wait_ge(s_const, 5)
            for u in range(4):
                unit(u, u % 2, u == 0)
                head_copies(4 + u)
            with act.Fori(2, UNITS // 2) as pair:
                unit(2 * pair, 0, False)
                unit(2 * pair + 1, 1, False)

        @block.vector
        def _(dve):
            V = nc.vector
            fence = V.drain

            def rstd(var, n, post=None):
                v, r, a = nw[:, 0, 0:n], nw[:, 3, 0:n], nw[:, 1, 0:n]
                half = nw[:, 2, 0:n].bitcast(i32)
                fence()
                V.tensor_scalar(v, var, EPS, None, ALU.add)
                fence()
                V.tensor_scalar(half, v.bitcast(i32), 1, None, ALU.logical_shift_right)
                fence()
                V.tensor_scalar(r.bitcast(i32), half, -1.0, float(0x5F3759DF), ALU.mult, ALU.add)
                for _ in range(4):
                    fence()
                    V.tensor_tensor(a, r, r, ALU.mult)
                    fence()
                    V.scalar_tensor_tensor(a, a, -0.5, v, ALU.mult, ALU.mult)
                    fence()
                    V.scalar_tensor_tensor(r, a, 1.5, r, ALU.add, ALU.mult)
                fence()
                return r

            def layer_norm(z, w, b):
                width = z.shape[-1]
                n = width // 512
                for i in range(n):
                    V.bn_stats(st[:, i, :], z[:, i * 512:(i + 1) * 512])
                fence()
                V.bn_aggr(mv[:, 0, :], st[:, 0:n, :].rearrange("p a b -> p (a b)"))
                r = rstd(mv[:, 0, 1:2], 1)
                V.tensor_scalar(z, z, mv[:, 0, 0:1], r, ALU.subtract, ALU.mult)
                fence()
                V.tensor_tensor(z, z, w, ALU.mult)
                fence()
                return V.tensor_tensor(z, z, b, ALU.add)

            def decay_strips():
                x0, neg, ab, e, z, z2, p, lo = (dec[:, i, :] for i in range(8))
                lg = dec[:, 8, :]
                den = dec[:, 9, :]
                dve.wait_ge(s_edec, 1)
                V.tensor_scalar(den, e, 2.0, None, ALU.add)
                fence()
                V.reciprocal(den, den)
                fence()
                V.tensor_tensor(z, e, den, ALU.mult)
                fence()
                V.tensor_tensor(z2, z, z, ALU.mult)
                fence()
                V.tensor_scalar(p, z2, 1.0 / 17, None, ALU.mult)
                for k in range(15, 1, -2):
                    fence()
                    V.scalar_tensor_tensor(p, p, 1.0 / k, z2, ALU.add, ALU.mult)
                V.tensor_scalar(lo, x0, 0.0, None, ALU.min)
                fence()
                V.scalar_tensor_tensor(p, p, 1.0, z, ALU.add, ALU.mult)
                fence()
                V.scalar_tensor_tensor(lg, p, -2.0, lo, ALU.mult, ALU.add)
                dve.wait_ge(s_const, 5)
                V.tensor_scalar(behind, ahead, -1.0, 0.0, ALU.mult, ALU.max)
                fence()
                V.tensor_scalar(ahead, ahead, 0.0, None, ALU.max)
                fence()
                for h in range(HEADS):
                    V.tensor_scalar(part, behind, lg[:, HEADS + h:HEADS + h + 1], None, ALU.mult)
                    fence()
                    V.scalar_tensor_tensor(strip[:, h, :], ahead, lg[:, h:h + 1], part,
                                           ALU.mult, ALU.add).then_inc(s_z, 1)
                    fence()

            dve.wait_ge(s_dec, 32)
            V.tensor_scalar(dec[:, 1, :], dec[:, 0, :], -1.0, None, ALU.mult)
            fence()
            V.tensor_tensor(dec[:, 2, :], dec[:, 0, :], dec[:, 1, :], ALU.max).then_inc(s_adec, 1)

            cos = ropet[:, :, 0, :]
            sin = ropet[:, :, 1, :]
            for kind, arg, by, b, n in JOBS:
                if kind == "wsT":
                    dve.wait_ge(s_gain, 64)
                    for t in range(NT):
                        dve.wait_ge(s_gv, t + 1)
                        layer_norm(vln[:, t, :], gains[:, 0, :], gains[:, 1, :]).then_inc(s_vln, 1)
                    decay_strips()
                if by != "dve":
                    continue
                dve.wait_ge(full[b], n + 1)
                bank = ps[:, b, :]
                bank4 = bank.rearrange("p (c n) -> p c n", c=4)
                if kind == "xT":
                    t = arg[0]
                    V.tensor_copy(xT[:, 4:8, t * P:(t + 1) * P], bank4).then_inc(free[b], 1)
                    fence().then_inc(s_xT, 1)
                elif kind == "keysT":
                    q = arg[0]
                    V.tensor_copy(keysT[:, 4 * q:4 * q + 4, :], bank4).then_inc(free[b], 1)
                    fence().then_inc(s_keysT, 1)
                elif kind == "mix":
                    h = arg[0]
                    bias = gains[:, 3, h * P:(h + 1) * P].unsqueeze(1).broadcast_to([P, NT, P])
                    t4 = tmp[:, h, :].rearrange("p (c n) -> p c n", c=NT)
                    V.tensor_tensor(t4, bank4, bias, ALU.add).then_inc(free[b], 1)
                    dve.wait_ge(s_gu, h + 1)
                    fence()
                    V.tensor_tensor(mixT[:, h, :], mixT[:, h, :], tmp[:, h, :], ALU.mult).then_inc(s_mix, 1)
                elif kind == "qk":
                    w, t = arg
                    if w == 0 and t == 0:
                        dve.wait_ge(s_rope, 16)
                    x1 = bank4[:, :, 0:64]
                    x2 = bank4[:, :, 64:128]
                    ct = cos[:, t, :].unsqueeze(1).broadcast_to([P, HEADS, 64])
                    sn = sin[:, t, :].unsqueeze(1).broadcast_to([P, HEADS, 64])
                    r4 = tmp[:, t % 2, :].rearrange("p (c n) -> p c n", c=HEADS)
                    if w or t >= 2:
                        dve.wait_ge(s_qkT, NT * w + t - 1)
                    a4 = tmp[:, 2, :].rearrange("p (c n) -> p c n", c=HEADS)
                    V.tensor_tensor(r4[:, :, 0:64], x1, ct, ALU.mult)
                    V.tensor_tensor(r4[:, :, 64:128], x2, ct, ALU.mult)
                    V.tensor_tensor(a4[:, :, 0:64], x2, sn, ALU.mult)
                    V.tensor_tensor(a4[:, :, 64:128], x1, sn, ALU.mult).then_inc(free[b], 1)
                    fence()
                    V.tensor_tensor(r4[:, :, 0:64], r4[:, :, 0:64], a4[:, :, 0:64], ALU.subtract)
                    V.tensor_tensor(r4[:, :, 64:128], r4[:, :, 64:128], a4[:, :, 64:128], ALU.add)
                    fence().then_inc(s_rot, 1)
                elif kind == "score":
                    h, m = arg
                    if m == 0:
                        dve.wait_ge(s_strip, h + 1)
                    c0 = SEQ - P - m * P
                    V.scalar_tensor_tensor(prob[h % 2][:, m, :], bank, SCALE, strip[:, h, c0:c0 + SEQ],
                                           ALU.mult, ALU.mult).then_inc(free[b], 1)
                    fence().then_inc(s_prob, 1)
                elif kind == "read":
                    h = arg[0]
                    o = rnorm[:, h, :].rearrange("p (c n) -> p c n", c=NT)
                    for c in range(NT):
                        V.bn_stats(st[:, c, :], bank4[:, c, :])
                    fence()
                    for c in range(NT):
                        V.bn_aggr(mv[:, c, :], st[:, c, :])
                    r = rstd(mv[:, :, 1], NT)
                    for c in range(NT):
                        last = V.tensor_scalar(o[:, c, :], bank4[:, c, :], mv[:, c, 0:1], r[:, c:c + 1],
                                               ALU.subtract, ALU.mult)
                    last.then_inc(free[b], 1)
                    fence()
                    V.tensor_tensor(o, o, gains[:, 2, h * P:(h + 1) * P].unsqueeze(1).broadcast_to([P, NT, P]),
                                    ALU.mult)
                    if h == 0:
                        dve.wait_ge(s_gate, NT)
                    fence()
                    V.tensor_tensor(o, o, gate[:, :, h * P:(h + 1) * P], ALU.mult).then_inc(s_rn, 1)
                elif kind == "out":
                    t, half = arg
                    z = xh[:, t * D + half * 512:t * D + half * 512 + 512]
                    V.scalar_tensor_tensor(z, z, ALPHA, bank, ALU.mult, ALU.add).then_inc(free[b], 1)
                    if half == 1:
                        if t == 0:
                            dve.wait_ge(s_ln, 32)
                        fence()
                        layer_norm(xh[:, t * D:(t + 1) * D], lnp[:, 0, :], lnp[:, 1, :]).then_inc(s_h, 1)

            def top16(src, values, index, spare):
                V.max(values[:, 0:8], src)
                fence()
                V.max_index(index[:, 0:8], values[:, 0:8], src)
                V.match_replace(spare, values[:, 0:8], src, NEG)
                fence()
                V.max(values[:, 8:16], spare)
                fence()
                V.max_index(index[:, 8:16], values[:, 8:16], spare)

            def choose(u, k):
                V.tensor_copy(sc[:, 0, :], S[:, bass.ts(u, 256)])
                fence()
                for p in range(2):
                    top16(sc[:, 0, p * NK:(p + 1) * NK], top[:, p, :], topi[:, p, :],
                          sc[:, 1, p * NK:(p + 1) * NK])
                fence()
                V.tensor_copy(topf[:], topi[:])
                a = top[:, 0, :].unsqueeze(2).broadcast_to([P, TOPK, TOPK])
                bb = top[:, 1, :].unsqueeze(1).broadcast_to([P, TOPK, TOPK])
                V.tensor_tensor(cand[:].rearrange("p (a b) -> p a b", a=TOPK), a, bb, ALU.add)
                fence()
                top16(cand[:], best[:, k, :], pos[:], sc[:, 0, :])
                fence()
                V.tensor_scalar(posab[:, 0, :], pos[:], 4, None, ALU.logical_shift_right)
                V.tensor_scalar(posab[:, 1, :], pos[:], 15, None, ALU.bitwise_and)
                V.tensor_scalar(negmax[:, k:k + 1], best[:, k, 0:1], -1.0, None, ALU.mult).then_inc(s_best, 1)
                fence()
                V.tensor_copy(posf[:], posab[:])
                fence()
                for p in range(2):
                    e3 = eq[:, p * 256:(p + 1) * 256].rearrange("p (k a) -> p k a", a=TOPK)
                    V.tensor_tensor(e3, posf[:, p, :].unsqueeze(2).broadcast_to([P, TOPK, TOPK]),
                                    iota16[:].unsqueeze(1).broadcast_to([P, TOPK, TOPK]), ALU.is_equal)
                fence()
                for p in range(2):
                    e3 = eq[:, p * 256:(p + 1) * 256].rearrange("p (k a) -> p k a", a=TOPK)
                    V.tensor_tensor(e3, e3, topf[:, p, :].unsqueeze(1).broadcast_to([P, TOPK, TOPK]), ALU.mult)
                fence()
                V.tensor_reduce(pick[:], eq.rearrange("p (q k a) -> p q k a", q=2, a=TOPK), AX.X, ALU.add)
                fence()
                V.scalar_tensor_tensor(eid[:, k, :], pick[:, 0, :], float(NK), pick[:, 1, :], ALU.mult, ALU.add)
                fence()

            def publish(k):
                V.tensor_copy(idx[:, k, :], eid[:, k, :]).then_inc(s_idx, 1)

            def add_unit(u, k, tile):
                dve.wait_ge(s_vexp, 16 * u + 16)
                yt = y[:, bass.ts(tile, D)]
                V.tensor_tensor(yt, yt, acc[k], ALU.add).then_inc(s_yadd, 1)

            def unit(u, k, tile, before, first=False, new_tile=False):
                if new_tile:
                    V.tensor_copy(hcur, xh[:, bass.ts(tile, D)])
                    fence()
                for e in range(TOPK):
                    dve.wait_ge(s_u[e % RING], 32 * u + 16 * (1 + e // RING))
                    V.tensor_tensor_reduce(out=urow[e % RING], in0=urow[e % RING], in1=hcur, scale=1.0,
                                           scalar=0.0, op0=ALU.mult, op1=ALU.add,
                                           accum_out=dots[:, k, e:e + 1]).then_inc(s_dot, 1)
                if not first:
                    add_unit(u - 1, 1 - k, before)
                publish(1 - k)
                dve.wait_ge(s_exp, u + 1)
                V.reciprocal(rsum[:, k:k + 1], esum[:, k:k + 1])
                fence()
                dve.wait_ge(s_gel, u + 1)
                V.scalar_tensor_tensor(wgt[:, k, :], gel[:, k, :], rsum[:, k:k + 1], eg[:, k, :],
                                       ALU.mult, ALU.mult).then_inc(s_wgt, 1)

            def finish_tile(tile):
                layer_norm(y[:, bass.ts(tile, D)], lnp[:, 0, :], lnp[:, 1, :]).then_inc(s_ln2, 1)
                fence()

            for u in range(2):
                dve.wait_ge(s_sc, 2 * u + 2)
                choose(u, u)
            publish(0)
            dve.wait_ge(s_y, NT)
            for u in range(4):
                unit(u, u % 2, 0, 0, first=u == 0, new_tile=u == 0)
                dve.wait_ge(s_sc, 2 * u + 6)
                choose(u + 2, u % 2)
            dve.wait_ge(s_sc, 2 * PH)
            dve.wait_ge(s_const, 5)

            def pair_of_units(pair, tile, before, new_tile=False):
                unit(2 * pair, 0, tile, before, new_tile=new_tile)
                choose(2 * pair + 2, 0)
                unit(2 * pair + 1, 1, tile, tile)
                choose(2 * pair + 3, 1)

            with dve.Fori(2, PH // 2) as pair:
                pair_of_units(pair, 0, 0)
            dve.wait_ge(s_ln, 64)
            with dve.Fori(1, NT) as tile:
                pair_of_units(tile * (PH // 2), tile, tile - 1, new_tile=True)
                finish_tile(tile - 1)
                with dve.Fori(1, PH // 2) as j:
                    pair_of_units(tile * (PH // 2) + j, tile, tile)
            add_unit(UNITS - 1, 1, NT - 1)
            fence()
            finish_tile(NT - 1)

        @block.tensor
        def _(pe):
            T = nc.tensor

            def group(g):
                pe.wait_ge(s_w[g % WRING], 16 * (g // WRING + 1))
                return wring[:, g % WRING, :, :]

            def product(dst, lhs, rhs, n):
                for i in range(n):
                    last = T.matmul(dst, lhs(i), rhs(i), start=(i == 0), stop=(i == n - 1))
                return last

            pe.wait_ge(s_const, 5)
            for kind, arg, by, b, n in JOBS:
                if n:
                    pe.wait_ge(free[b], n)
                bank = ps[:, b, :]
                bank4 = bank.rearrange("p (c n) -> p c n", c=4)
                used = None
                if kind == "xT":
                    t, half = arg
                    if half == 0:
                        pe.wait_ge(s_x[t], 16)
                    for i in range(4):
                        k = 4 * half + i
                        last = T.transpose(bank4[:, i, :], xh[:, t * D + k * P:t * D + (k + 1) * P], ident[:])
                elif kind == "gv":
                    t = arg[0]
                    if t == 0:
                        pe.wait_ge(s_xT, 2 * NT)
                    w = group(GV)
                    last = product(bank, lambda k: xT[:, k, t * P:(t + 1) * P], lambda k: w[:, k, :], KC)
                    used = t == NT - 1
                elif kind == "wsT":
                    pe.wait_ge(s_ws, 16)
                    for h in range(HEADS):
                        last = T.transpose(bank4[:, h, :], ws_raw[:, h, :], ident[:])
                elif kind == "keysT":
                    if arg[0] == 0:
                        pe.wait_ge(s_keys, 16)
                    for i in range(4):
                        last = T.transpose(bank4[:, i, :], keys_raw[:, 4 * arg[0] + i, :], ident[:])
                elif kind == "gu":
                    c = arg[0]
                    w = group(GU)
                    last = product(bank, lambda k: w[:, k, c * P:(c + 1) * P], lambda k: xT[:, k, :], KC)
                    used = c == 3
                elif kind == "mix":
                    h = arg[0]
                    if h == 0:
                        pe.wait_ge(s_vln, NT)
                        pe.wait_ge(s_wsT, 1)
                    for c in range(NT):
                        last = T.matmul(bank4[:, c, :], vln[:, c, h * P:(h + 1) * P], wsT[:, h, :],
                                        start=True, stop=True)
                elif kind == "qk":
                    w_, t = arg
                    w = group(GQ + w_)
                    last = product(bank, lambda k: xT[:, k, t * P:(t + 1) * P], lambda k: w[:, k, :], KC)
                    used = t == NT - 1
                elif kind == "qkT":
                    w_, t = arg
                    pe.wait_ge(s_rot, NT * w_ + t + 1)
                    for h in range(HEADS):
                        last = T.transpose(bank4[:, h, :], tmp[:, t % 2, h * P:(h + 1) * P], ident[:])
                elif kind in ("rv", "rg"):
                    t = arg[0]
                    w = group(GRV if kind == "rv" else GG)
                    last = product(bank, lambda k: xT[:, k, t * P:(t + 1) * P], lambda k: w[:, k, :], KC)
                    used = t == NT - 1
                elif kind == "score":
                    h, m = arg
                    if h == 0 and m == 0:
                        pe.wait_ge(s_qkT, 2 * NT)
                    last = T.matmul(bank, qkT[:, 1, h, m * P:(m + 1) * P], qkT[:, 0, h, :], start=True, stop=True)
                elif kind == "read":
                    h = arg[0]
                    if h == 0:
                        pe.wait_ge(s_rv, NT)
                    pe.wait_ge(s_prob, NT * (h + 1))
                    for c in range(NT):
                        last = product(bank4[:, c, :], lambda m: prob[h % 2][:, m, c * P:(c + 1) * P],
                                       lambda m: rv[:, m, h * P:(h + 1) * P], NT)
                elif kind == "rT":
                    h = arg[0]
                    pe.wait_ge(s_rn, h + 1)
                    for c in range(NT):
                        last = T.transpose(bank4[:, c, :], rnorm[:, h, c * P:(c + 1) * P], ident[:])
                elif kind == "out":
                    t, half = arg
                    if t == 0 and half == 0:
                        pe.wait_ge(s_mix, HEADS)
                        pe.wait_ge(s_rT, HEADS)
                    w = group(GO0 + half)
                    last = product(bank, lambda k: mixT[:, k, t * P:(t + 1) * P], lambda k: w[:, k, :], KC)
                elif kind == "hT":
                    t, half = arg
                    if half == 0:
                        pe.wait_ge(s_h, t + 1)
                    for i in range(4):
                        k = 4 * half + i
                        last = T.transpose(bank4[:, i, :], xh[:, t * D + k * P:t * D + (k + 1) * P], ident[:])
                last.then_inc(full[b], 1)
                if used:
                    T.drain().then_inc(s_wdone, 1)
                if kind == "out" and arg == (NT - 1, 1):
                    T.drain().then_inc(s_wdone, 2)
                if kind == "score" and arg == (HEADS - 1, NT - 1):
                    T.drain().then_inc(s_scored, 1)

            def head(h):
                for kind, (_, p), _, b, n in HJOBS[h]:
                    pe.wait_ge(free[b], n)
                    if kind == "query":
                        if p == 0:
                            pe.wait_ge(s_wq[h % 2], 16 * (h // 2 + 1))
                            if h == 0:
                                pe.wait_ge(s_hT, 2 * NT)
                        last = product(ps[:, b, :], lambda k: wq[:, h % 2, k, p * P:(p + 1) * P],
                                       lambda k: xT[:, k, :], KC)
                        last.then_inc(full[b], 1)
                        if p == 1:
                            T.drain().then_inc(s_wqd, 1)
                    else:
                        pe.wait_ge(s_qh, 2 * h + p + 1)
                        if h == 0 and p == 0:
                            pe.wait_ge(s_keysT, 4)
                        for t in range(NT):
                            last = T.matmul(ps[:, b, t * P:(t + 1) * P], qh[:, h % 2, p, t * P:(t + 1) * P],
                                            keysT[:, 2 * h + p, :], start=True, stop=True)
                        last.then_inc(full[b], 1)

            def unit(u, k, first):
                if not first:
                    pe.wait_ge(s_yadd, u - 1)
                for e in range(TOPK):
                    pe.wait_ge(s_v[e % RING], 32 * u + 16 * (1 + e // RING))
                    pe.wait_ge(s_diag, 16 * u + e + 1)
                    for half in range(2):
                        last = T.matmul(acc[k][:, half * 512:(half + 1) * 512], diag[:, e % NDIAG, :],
                                        vrow[e % RING][:, half * 512:(half + 1) * 512],
                                        start=(e == 0), stop=(e == TOPK - 1))
                    last.then_inc(s_vexp, 1)

            for h in range(4):
                head(h)
            for b in range(4):
                pe.wait_ge(free[b], USED[b])
            for u in range(4):
                unit(u, u % 2, u < 2)
                head(4 + u)
            with pe.Fori(2, UNITS // 2) as pair:
                unit(2 * pair, 0, False)
                unit(2 * pair + 1, 1, False)


_INS = ["x", "w_in", "sgu_ln_w", "sgu_ln_b", "sgu_w_s", "sgu_b", "ret_decay_fwd", "ret_decay_bwd", "ret_gn_w",
        "w_out", "ln1_w", "ln1_b", "peer_w_q", "peer_sub_keys", "peer_u", "peer_v", "ln2_w", "ln2_b"]


def kernel(**inputs):
    import numpy as _np
    import concourse.bacc as _bacc
    from concourse import mybir as _mybir
    from concourse.bass_utils import run_bass_kernel_spmd as _run

    nc = _bacc.Bacc("TRN2", target_bir_lowering=False, num_devices=1)
    arrays, args = {}, []
    for name in _INS:
        a = _np.ascontiguousarray(inputs[name])
        arrays[f"in_{name}_dram"] = a
        args.append(nc.dram_tensor(f"in_{name}_dram", a.shape, _mybir.dt.from_np(a.dtype), kind="ExternalInput").ap())
    half = P // 2
    inv = _np.float32(10000.0) ** (-_np.arange(half, dtype=_np.float32) / _np.float32(half))
    ang = _np.arange(SEQ, dtype=_np.float32)[:, None] * inv[None, :].astype(_np.float32)
    table = _np.stack([_np.cos(ang), _np.sin(ang)], axis=1).astype(_np.float32)
    table = _np.ascontiguousarray(table.reshape(NT, P, 2, half).transpose(1, 0, 2, 3))
    arrays["rope_dram"] = table
    args.append(nc.dram_tensor("rope_dram", table.shape, _mybir.dt.float32, kind="ExternalInput").ap())
    out = nc.dram_tensor("out_dram", (1, SEQ, D), _mybir.dt.float32, kind="ExternalOutput").ap()
    layer(nc, *args, out)
    r = _run(nc, [arrays], core_ids=[0])
    return r.results[0]["out_dram"]
```

```python
import numpy as np
import concourse.bass as bass
from concourse import mybir
from contextlib import ExitStack

P = 128
SEQ, D = 512, 1024
NT = SEQ // P
KC = D // P
GW = 512
HEADS = 4
PH, TOPK, NK = 8, 16, 128
UNITS = NT * PH
RING = 8
NDIAG = 8
ALPHA = 2.0 ** 0.25
EPS = 1e-5
SCALE = float(P) ** -0.5
STRIP = 2 * SEQ - P
NEG = -3.0e38
GV, GU, GQ, GK, GRV, GG, GO0, GO1 = range(8)
GROUP_COL = {GV: 512, GU: 0, GQ: 1024, GK: 1536, GRV: 2048, GG: 2560, GO0: 0, GO1: 512}
WRING = 4


def phase_a_jobs():
    jobs = []

    def add(kind, *arg, by):
        jobs.append((kind, arg, by))

    for t in range(NT):
        add("xT", t, 0, by="act")
        add("xT", t, 1, by="dve")
    for t in range(NT):
        add("gv", t, by="act")
    add("wsT", by="act")
    for q in range(4):
        add("keysT", q, by="dve")
    for c in range(4):
        add("gu", c, by="act")
    for h in range(HEADS):
        add("mix", h, by="dve")
    for w, kind in ((0, "rot"), (1, "rot")):
        for t in range(NT):
            add("qk", w, t, by="dve")
            if t:
                add("qkT", w, t - 1, by="act")
        add("qkT", w, NT - 1, by="act")
    for t in range(NT):
        add("rv", t, by="act")
    def score(h):
        for m in range(NT):
            add("score", h, m, by="dve")

    score(0)
    add("rg", 0, by="act")
    score(1)
    add("rg", 1, by="act")
    add("read", 0, by="dve")
    add("rg", 2, by="act")
    score(2)
    add("read", 1, by="dve")
    add("rg", 3, by="act")
    add("rT", 0, by="act")
    score(3)
    add("read", 2, by="dve")
    add("rT", 1, by="act")
    add("read", 3, by="dve")
    add("rT", 2, by="act")
    add("rT", 3, by="act")
    for t in range(NT):
        add("out", t, 0, by="dve")
        add("out", t, 1, by="dve")
        if t:
            add("hT", t - 1, 0, by="act")
            add("hT", t - 1, 1, by="act")
    add("hT", NT - 1, 0, by="act")
    add("hT", NT - 1, 1, by="act")
    placed, used = [], [0] * 8
    for i, (kind, arg, by) in enumerate(jobs):
        b = i % 8
        placed.append((kind, arg, by, b, used[b]))
        used[b] += 1
    return placed, used


def head_jobs(used):
    out, used = [], list(used)
    for h in range(PH):
        this = []
        for kind, first in (("query", 4), ("keys", 6)):
            for p in range(2):
                this.append((kind, (h, p), "act", first + p, used[first + p]))
                used[first + p] += 1
        out.append(this)
    return out


def layer(nc, x, w_in, sgu_ln_w, sgu_ln_b, sgu_w_s, sgu_b, decay_fwd, decay_bwd, gn_w, w_out, ln1_w, ln1_b,
          w_q, sub_keys, peer_u, peer_v, ln2_w, ln2_b, rope, out):
    f32, i32 = mybir.dt.float32, mybir.dt.int32
    u32 = mybir.dt.uint32
    ALU, ACT = mybir.AluOpType, mybir.ActivationFunctionType
    AX = mybir.AxisListType

    JOBS, USED = phase_a_jobs()
    HJOBS = head_jobs(USED)

    ctx = ExitStack()
    with ctx:
        def sb(name, shape, dt=f32):
            return ctx.enter_context(nc.sbuf_tensor(name, shape, dt))

        def sem(name):
            return ctx.enter_context(nc.semaphore(name))

        big = sb("big", [P, 2 * RING * D])
        wring = big[:, :].rearrange("p (s k n) -> p s k n", s=WRING, k=KC)
        rows = big[:, :].rearrange("p (s n) -> p s n", n=D)
        urow = [rows[:, s, :] for s in range(RING)]
        vrow = [rows[:, RING + s, :] for s in range(RING)]
        xh = sb("xh", [P, NT * D])
        xT = sb("xT", [P, KC, SEQ])
        prob1 = big[:, 0:2048].rearrange("p (m n) -> p m n", m=NT)
        rnorm = big[:, 2048:4096].rearrange("p (h n) -> p h n", h=HEADS)
        y = sb("y", [P, NT * D])
        strip = y[:, 0:HEADS * STRIP].rearrange("p (h n) -> p h n", h=HEADS)
        S = sb("S", [P, UNITS * 256 + 512])
        S4 = S[:, 0:UNITS * 256].rearrange("p (t q n) -> p t q n", t=NT, q=2 * PH)
        rv = S[:, 0:2048].rearrange("p (t n) -> p t n", t=NT)
        gate = S[:, 2048:4096].rearrange("p (t n) -> p t n", t=NT)
        keys_raw = S[:, 2048:4096].rearrange("p (q n) -> p q n", q=2 * PH)
        gains = S[:, 4096:6144].rearrange("p (g n) -> p g n", g=4)
        prob0 = S[:, 6144:8192].rearrange("p (m n) -> p m n", m=NT)
        ws_raw = S[:, 6144:6656].rearrange("p (h n) -> p h n", h=HEADS)
        tmp = S[:, 6144:8192].rearrange("p (m n) -> p m n", m=NT)
        prob = [prob0, prob1]
        mixT = sb("mixT", [P, KC, SEQ])
        vln = mixT[:, 4:8, :]
        mix1 = mixT[:, :, :].rearrange("p k n -> p (k n)")
        hcur = mix1[:, 0:D]
        qh = mix1[:, D:D + 2 * 1024].rearrange("p (s q n) -> p s q n", s=2, q=2)
        eq = mix1[:, 3 * D:3 * D + 512]
        sc = mix1[:, 3 * D + 512:4 * D].rearrange("p (a n) -> p a n", a=2)
        qkT = sb("qkT", [P, 2, HEADS, SEQ])
        qk1 = qkT[:, :, :, :].rearrange("p a h n -> p (a h n)")
        ahead, behind, part = (qk1[:, 1024 * i:1024 * i + STRIP] for i in range(3))
        wq = qk1.rearrange("p (s k n) -> p s k n", s=2, k=KC)
        lnp = sb("lnp", [P, 2, D])
        keysT = sb("keysT", [P, 2 * PH, NK])
        wsT = sb("wsT", [P, HEADS, P])
        ropet = sb("ropet", [P, NT, 2, 64])
        ident = sb("ident", [P, P])
        diag = sb("diag", [P, NDIAG, P])
        iota16 = sb("iota16", [P, TOPK])
        dec = sb("dec", [P, 10, 2 * HEADS])
        st = sb("st", [P, 4, 6])
        mv = sb("mv", [P, 4, 2])
        nw = sb("nw", [P, 4, 4])
        cand = sb("cand", [P, 256])
        top = sb("top", [P, 2, TOPK])
        topi = sb("topi", [P, 2, TOPK], u32)
        topf = sb("topf", [P, 2, TOPK])
        best = sb("best", [P, 2, TOPK])
        pos = sb("pos", [P, TOPK], u32)
        posab = sb("posab", [P, 2, TOPK], u32)
        posf = sb("posf", [P, 2, TOPK])
        pick = sb("pick", [P, 2, TOPK])
        idxu = sb("idxu", [P, 2, TOPK], i32)
        idxv = sb("idxv", [P, 2, TOPK], i32)
        negmax = sb("negmax", [P, 2])
        esum = sb("esum", [P, 2])
        rsum = sb("rsum", [P, 2])
        eg = sb("eg", [P, 2, TOPK])
        dots = sb("dots", [P, 2, TOPK])
        gel = sb("gel", [P, 2, TOPK])
        wgt = sb("wgt", [P, 2, TOPK])
        ps = ctx.enter_context(nc.psum_tensor("ps", [P, 8, 512], f32))
        acc = [ps[:, 2 * k:2 * k + 2, :].rearrange("p a n -> p (a n)") for k in range(2)]

        full = [sem(f"bank_full{b}") for b in range(8)]
        free = [sem(f"bank_free{b}") for b in range(8)]
        s_x = [sem(f"x_loaded{t}") for t in range(NT)]
        s_w = [sem(f"weights_loaded{s}") for s in range(WRING)]
        s_wdone = sem("weights_used")
        s_ws, s_keys, s_rope = sem("ws_loaded"), sem("keys_loaded"), sem("rope_loaded")
        s_gain, s_dec, s_ln = sem("gains_loaded"), sem("decay_loaded"), sem("ln_loaded")
        s_const = sem("constants_ready")
        s_xT = sem("xT_ready")
        s_wsT, s_keysT = sem("wsT_ready"), sem("keysT_ready")
        s_gv, s_vln = sem("gelu_v_ready"), sem("vln_ready")
        s_gu, s_mix = sem("gelu_u_ready"), sem("gating_ready")
        s_adec, s_edec, s_z, s_strip = sem("absdecay_ready"), sem("expdecay_ready"), sem("logstrip_ready"), sem("strip_ready")
        s_rot, s_qkT = sem("rotated_ready"), sem("qkT_ready")
        s_rv, s_gate = sem("rv_ready"), sem("gate_ready")
        s_scored = sem("scores_done")
        s_norm = sem("normalised_ready")
        s_gg = sem("gate_times_gain_ready")
        s_prob, s_rn, s_rT = sem("prob_ready"), sem("retention_ready"), sem("retentionT_ready")
        s_h, s_hT, s_y = sem("h_ready"), sem("hT_ready"), sem("y_started")
        s_wq = [sem(f"wq_loaded{s}") for s in range(2)]
        s_wqd = sem("wq_used")
        s_qh, s_sc = sem("query_ready"), sem("key_scores_ready")
        s_best, s_exp = sem("best_ready"), sem("exp_ready")
        s_idxu, s_idxv = sem("indices_u_ready"), sem("indices_v_ready")
        s_u = [sem(f"urow_gathered{s}") for s in range(RING)]
        s_v = [sem(f"vrow_gathered{s}") for s in range(RING)]
        s_dot, s_gel, s_wgt = sem("dots_done"), sem("gelu_ready"), sem("expert_weights_ready")
        s_diag, s_vexp = sem("diag_ready"), sem("experts_added")
        s_yadd = sem("unit_added")
        s_ln2, s_out = sem("output_ready"), sem("output_stored")

        peer_u2, peer_v2 = peer_u[0], peer_v[0]
        w_in3 = w_in[0].rearrange("(k p) n -> p k n", p=P)
        w_out3 = w_out[0].rearrange("(k p) n -> p k n", p=P)
        w_q3 = w_q[0].rearrange("(k p) n -> p k n", p=P)
        out3 = out[0].rearrange("(t p) n -> p t n", p=P)

        block = ctx.enter_context(nc.Block())

        @block.sync
        def _(sp):
            def load_group(g):
                if g >= WRING:
                    sp.wait_ge(s_wdone, g - WRING + 1)
                src = w_out3 if g >= GO0 else w_in3
                c = GROUP_COL[g]
                sp.dma_start(wring[:, g % WRING, :, :], src[:, :, c:c + GW]).then_inc(s_w[g % WRING], 16)

            for t in range(NT):
                sp.dma_start(xh[:, t * D:(t + 1) * D], x[0, t * P:(t + 1) * P, :]).then_inc(s_x[t], 16)
            for g in range(8):
                load_group(g)
            sp.wait_ge(s_scored, 1)
            for h in range(PH):
                if h >= 2:
                    sp.wait_ge(s_wqd, h - 1)
                sp.dma_start(wq[:, h % 2, :, :], w_q3[:, :, h * 256:(h + 1) * 256]).then_inc(s_wq[h % 2], 16)
                if h == 1:
                    sp.wait_ge(s_h, NT)
                    sp.dma_start(lnp[:, 0, :], ln2_w[0].partition_broadcast(P)).then_inc(s_ln, 16)
                    sp.dma_start(lnp[:, 1, :], ln2_b[0].partition_broadcast(P)).then_inc(s_ln, 16)
            for t in range(NT):
                sp.wait_ge(s_ln2, t + 1)
                sp.dma_start(out3[:, t, :], y[:, t * D:(t + 1) * D]).then_inc(s_out, 16)
            sp.wait_ge(s_out, 16 * NT)

        @block.gpsimd
        def _(pool):
            nc.gpsimd.memset(ident[:], 0.0).then_inc(s_const, 1)
            nc.gpsimd.memset(S[:, UNITS * 256:], 0.0).then_inc(s_const, 1)
            nc.gpsimd.iota(iota16[:], pattern=[[1, TOPK]], base=0, channel_multiplier=0,
                           allow_small_or_imprecise_dtypes=True).then_inc(s_const, 1)
            nc.gpsimd.iota(ahead, pattern=[[1, STRIP]], base=-(SEQ - P), channel_multiplier=-1,
                           allow_small_or_imprecise_dtypes=True).then_inc(s_const, 1)
            pool.wait_ge(s_const, 1)
            nc.gpsimd.affine_select(out=ident[:], in_=ident[:], compare_op=ALU.not_equal, fill=1.0, base=0,
                                    pattern=[[-1, P]], channel_multiplier=1).then_inc(s_const, 1)
            pool.wait_ge(s_gain, 64)
            for t in range(NT):
                pool.wait_ge(s_gate, t + 1)
                nc.gpsimd.tensor_tensor(gate[:, t, :], gate[:, t, :], gains[:, 2, :], ALU.mult).then_inc(s_gg, 1)
            pool.wait_ge(s_gg, NT)
            for h in range(HEADS):
                pool.wait_ge(s_norm, h + 1)
                o = rnorm[:, h, :].rearrange("p (c n) -> p c n", c=NT)
                nc.gpsimd.tensor_tensor(o, o, gate[:, :, h * P:(h + 1) * P], ALU.mult).then_inc(s_rn, 1)
            pool.wait_ge(s_wdone, 8)

            def gather(table, row, index, e, signal):
                nc.gpsimd.indirect_dma_start(row[e % RING], None, table,
                                             bass.IndirectOffsetOnAxis(ap=index[:, e:e + 1], axis=0)
                                             ).then_inc(signal[e % RING], 16)

            def block_of_gathers(u, k, first=False, last=False):
                pool.wait_ge(s_idxv, u + 1)
                pool.nop(nofuse=True)
                if not last:
                    pool.wait_ge(s_idxu, u + 2)
                    pool.nop(nofuse=True)
                for e in range(TOPK):
                    if e % 4 == 0 and not (first and e < RING):
                        pool.wait_ge(s_vexp, 16 * u + e + 4 - RING)
                        pool.nop(nofuse=True)
                    gather(peer_v2, vrow, idxv[:, k, :], e, s_v)
                    if not last:
                        if e % 4 == 0:
                            pool.wait_ge(s_dot, 16 * u + 16 + e + 4 - RING)
                            pool.nop(nofuse=True)
                        gather(peer_u2, urow, idxu[:, 1 - k, :], e, s_u)

            pool.wait_ge(s_idxu, 1)
            for e in range(TOPK):
                if e >= RING and e % 4 == 0:
                    pool.wait_ge(s_dot, e + 4 - RING)
                gather(peer_u2, urow, idxu[:, 0, :], e, s_u)
            block_of_gathers(0, 0, first=True)
            block_of_gathers(1, 1)
            with pool.Fori(1, UNITS // 2 - 1) as pair:
                block_of_gathers(2 * pair, 0)
                block_of_gathers(2 * pair + 1, 1)
            block_of_gathers(UNITS - 2, 0)
            block_of_gathers(UNITS - 1, 1, last=True)

        @block.scalar
        def _(act):
            A = nc.scalar

            def copy(dst, src):
                return A.activation(dst, src, ACT.Copy)

            act.dma_start(dec[:, 0, 0:HEADS], decay_fwd[0].partition_broadcast(P)).then_inc(s_dec, 16)
            act.dma_start(dec[:, 0, HEADS:], decay_bwd[0].partition_broadcast(P)).then_inc(s_dec, 16)
            act.dma_start(gains[:, 0, :], sgu_ln_w[0].partition_broadcast(P)).then_inc(s_gain, 16)
            act.dma_start(gains[:, 1, :], sgu_ln_b[0].partition_broadcast(P)).then_inc(s_gain, 16)
            act.dma_start(gains[:, 2, :], gn_w[0].partition_broadcast(P)).then_inc(s_gain, 16)
            act.dma_start(gains[:, 3, :], sgu_b[0].rearrange("h l -> (h l)").partition_broadcast(P)).then_inc(s_gain, 16)
            act.dma_start(ws_raw, sgu_w_s[0].rearrange("h l m -> l h m")).then_inc(s_ws, 16)
            act.dma_start(keys_raw, sub_keys[0].rearrange("h q n d -> n (h q) d")).then_inc(s_keys, 16)
            act.dma_start(ropet[:], rope).then_inc(s_rope, 16)
            act.dma_start(lnp[:, 0, :], ln1_w[0].partition_broadcast(P)).then_inc(s_ln, 16)
            act.dma_start(lnp[:, 1, :], ln1_b[0].partition_broadcast(P)).then_inc(s_ln, 16)

            act.wait_ge(s_adec, 1)
            A.activation(dec[:, 3, :], dec[:, 2, :], ACT.Exp, scale=-1.0).then_inc(s_edec, 1)
            done_h = 0
            for kind, arg, by, b, n in JOBS:
                if by != "act":
                    continue
                act.wait_ge(full[b], n + 1)
                bank = ps[:, b, :]
                bank4 = bank.rearrange("p (c n) -> p c n", c=4)
                if kind == "xT":
                    t = arg[0]
                    copy(xT[:, 0:4, t * P:(t + 1) * P], bank4).then_inc(free[b], 1)
                    A.drain().then_inc(s_xT, 1)
                elif kind == "gv":
                    A.activation(vln[:, arg[0], :], bank, ACT.Gelu).then_inc(free[b], 1)
                    A.drain().then_inc(s_gv, 1)
                elif kind == "wsT":
                    copy(wsT[:], bank4).then_inc(free[b], 1)
                    A.drain().then_inc(s_wsT, 1)
                elif kind == "gu":
                    A.activation(mixT[:, arg[0], :], bank, ACT.Gelu).then_inc(free[b], 1)
                    A.drain().then_inc(s_gu, 1)
                    if arg[0] == 3:
                        for h in range(HEADS):
                            act.wait_ge(s_z, h + 1)
                            A.activation(strip[:, h, :], strip[:, h, :], ACT.Exp).then_inc(s_strip, 1)
                elif kind == "qkT":
                    w, t = arg
                    copy(qkT[:, w, :, t * P:(t + 1) * P], bank4).then_inc(free[b], 1)
                    A.drain().then_inc(s_qkT, 1)
                elif kind == "rv":
                    copy(rv[:, arg[0], :], bank).then_inc(free[b], 1)
                    A.drain().then_inc(s_rv, 1)
                elif kind == "rg":
                    A.activation(gate[:, arg[0], :], bank, ACT.Silu).then_inc(free[b], 1)
                    A.drain().then_inc(s_gate, 1)
                elif kind == "rT":
                    copy(mixT[:, 4 + arg[0], :], bank).then_inc(free[b], 1)
                    A.drain().then_inc(s_rT, 1)
                elif kind == "hT":
                    t, half = arg
                    copy(xT[:, 4 * half:4 * half + 4, t * P:(t + 1) * P], bank4).then_inc(free[b], 1)
                    A.drain().then_inc(s_hT, 1)
                    if half == 1:
                        A.activation(y[:, t * D:(t + 1) * D], xh[:, t * D:(t + 1) * D], ACT.Copy,
                                     scale=ALPHA).then_inc(s_y, 1)

            def head_copies(h):
                for kind, (_, p), _, b, n in HJOBS[h]:
                    act.wait_ge(full[b], n + 1)
                    if kind == "query":
                        copy(qh[:, h % 2, p, :], ps[:, b, :]).then_inc(free[b], 1)
                        A.drain().then_inc(s_qh, 1)
                    else:
                        copy(S4[:, :, 2 * h + p, :],
                             ps[:, b, :].rearrange("p (c n) -> p c n", c=4)).then_inc(free[b], 1)
                        A.drain().then_inc(s_sc, 1)

            def exps(u, k):
                act.wait_ge(s_best, u + 1)
                A.activation(eg[:, k, :], best[:, k, :], ACT.Exp, bias=negmax[:, k:k + 1],
                             accum_out=esum[:, k:k + 1]).then_inc(s_exp, 1)

            def unit(u, k, first):
                exps(u + 1, 1 - k)
                act.wait_ge(s_dot, 16 * u + 16)
                A.activation(gel[:, k, :], dots[:, k, :], ACT.Gelu).then_inc(s_gel, 1)
                act.wait_ge(s_wgt, u + 1)
                for e in range(TOPK):
                    if e % 4 == 0 and not (first and e < NDIAG):
                        act.wait_ge(s_vexp, 16 * u + e + 4 - NDIAG)
                    A.activation(diag[:, e % NDIAG, :], ident[:], ACT.Copy,
                                 scale=wgt[:, k, e:e + 1]).then_inc(s_diag, 1)

            for h in range(3):
                head_copies(h)
                if h == 0:
                    exps(0, 0)
            act.wait_ge(s_const, 5)
            for u in range(6):
                unit(u, u % 2, u == 0)
                if u < 5:
                    head_copies(3 + u)
            with act.Fori(3, UNITS // 2) as pair:
                unit(2 * pair, 0, False)
                unit(2 * pair + 1, 1, False)

        @block.vector
        def _(dve):
            V = nc.vector
            fence = V.drain

            def rstd(var, n, post=None):
                v, r, a = nw[:, 0, 0:n], nw[:, 3, 0:n], nw[:, 1, 0:n]
                half = nw[:, 2, 0:n].bitcast(i32)
                fence()
                V.tensor_scalar(v, var, EPS, None, ALU.add)
                fence()
                V.tensor_scalar(half, v.bitcast(i32), 1, None, ALU.logical_shift_right)
                fence()
                V.tensor_scalar(r.bitcast(i32), half, -1.0, float(0x5F3759DF), ALU.mult, ALU.add)
                for _ in range(3):
                    fence()
                    V.tensor_tensor(a, r, r, ALU.mult)
                    fence()
                    V.scalar_tensor_tensor(a, a, -0.5, v, ALU.mult, ALU.mult)
                    fence()
                    V.scalar_tensor_tensor(r, a, 1.5, r, ALU.add, ALU.mult)
                fence()
                return r

            def layer_norm(z, w, b):
                width = z.shape[-1]
                n = width // 512
                for i in range(n):
                    V.bn_stats(st[:, i, :], z[:, i * 512:(i + 1) * 512])
                fence()
                V.bn_aggr(mv[:, 0, :], st[:, 0:n, :].rearrange("p a b -> p (a b)"))
                r = rstd(mv[:, 0, 1:2], 1)
                V.tensor_scalar(z, z, mv[:, 0, 0:1], r, ALU.subtract, ALU.mult)
                fence()
                V.tensor_tensor(z, z, w, ALU.mult)
                fence()
                return V.tensor_tensor(z, z, b, ALU.add)

            def decay_strips():
                x0, neg, ab, e, z, z2, p, lo = (dec[:, i, :] for i in range(8))
                lg = dec[:, 8, :]
                den = dec[:, 9, :]
                dve.wait_ge(s_edec, 1)
                V.tensor_scalar(den, e, 2.0, None, ALU.add)
                fence()
                V.reciprocal(den, den)
                fence()
                V.tensor_tensor(z, e, den, ALU.mult)
                fence()
                V.tensor_tensor(z2, z, z, ALU.mult)
                fence()
                V.tensor_scalar(p, z2, 1.0 / 17, None, ALU.mult)
                for k in range(15, 1, -2):
                    fence()
                    V.scalar_tensor_tensor(p, p, 1.0 / k, z2, ALU.add, ALU.mult)
                V.tensor_scalar(lo, x0, 0.0, None, ALU.min)
                fence()
                V.scalar_tensor_tensor(p, p, 1.0, z, ALU.add, ALU.mult)
                fence()
                V.scalar_tensor_tensor(lg, p, -2.0, lo, ALU.mult, ALU.add)
                dve.wait_ge(s_const, 5)
                V.tensor_scalar(behind, ahead, -1.0, 0.0, ALU.mult, ALU.max)
                fence()
                V.tensor_scalar(ahead, ahead, 0.0, None, ALU.max)
                fence()
                for h in range(HEADS):
                    V.tensor_scalar(part, behind, lg[:, HEADS + h:HEADS + h + 1], None, ALU.mult)
                    fence()
                    V.scalar_tensor_tensor(strip[:, h, :], ahead, lg[:, h:h + 1], part,
                                           ALU.mult, ALU.add).then_inc(s_z, 1)
                    fence()

            dve.wait_ge(s_dec, 32)
            V.tensor_scalar(dec[:, 1, :], dec[:, 0, :], -1.0, None, ALU.mult)
            fence()
            V.tensor_tensor(dec[:, 2, :], dec[:, 0, :], dec[:, 1, :], ALU.max).then_inc(s_adec, 1)

            cos = ropet[:, :, 0, :]
            sin = ropet[:, :, 1, :]
            for kind, arg, by, b, n in JOBS:
                if kind == "wsT":
                    dve.wait_ge(s_gain, 64)
                    for t in range(NT):
                        dve.wait_ge(s_gv, t + 1)
                        layer_norm(vln[:, t, :], gains[:, 0, :], gains[:, 1, :]).then_inc(s_vln, 1)
                    decay_strips()
                if by != "dve":
                    continue
                dve.wait_ge(full[b], n + 1)
                bank = ps[:, b, :]
                bank4 = bank.rearrange("p (c n) -> p c n", c=4)
                if kind == "xT":
                    t = arg[0]
                    V.tensor_copy(xT[:, 4:8, t * P:(t + 1) * P], bank4).then_inc(free[b], 1)
                    fence().then_inc(s_xT, 1)
                elif kind == "keysT":
                    q = arg[0]
                    V.tensor_copy(keysT[:, 4 * q:4 * q + 4, :], bank4).then_inc(free[b], 1)
                    fence().then_inc(s_keysT, 1)
                elif kind == "mix":
                    h = arg[0]
                    bias = gains[:, 3, h * P:(h + 1) * P].unsqueeze(1).broadcast_to([P, NT, P])
                    t4 = tmp[:, h, :].rearrange("p (c n) -> p c n", c=NT)
                    V.tensor_tensor(t4, bank4, bias, ALU.add).then_inc(free[b], 1)
                    dve.wait_ge(s_gu, h + 1)
                    fence()
                    V.tensor_tensor(mixT[:, h, :], mixT[:, h, :], tmp[:, h, :], ALU.mult).then_inc(s_mix, 1)
                elif kind == "qk":
                    w, t = arg
                    if w == 0 and t == 0:
                        dve.wait_ge(s_rope, 16)
                    x1 = bank4[:, :, 0:64]
                    x2 = bank4[:, :, 64:128]
                    ct = cos[:, t, :].unsqueeze(1).broadcast_to([P, HEADS, 64])
                    sn = sin[:, t, :].unsqueeze(1).broadcast_to([P, HEADS, 64])
                    r4 = tmp[:, t % 2, :].rearrange("p (c n) -> p c n", c=HEADS)
                    if w or t >= 2:
                        dve.wait_ge(s_qkT, NT * w + t - 1)
                    a4 = tmp[:, 2, :].rearrange("p (c n) -> p c n", c=HEADS)
                    V.tensor_tensor(r4[:, :, 0:64], x1, ct, ALU.mult)
                    V.tensor_tensor(r4[:, :, 64:128], x2, ct, ALU.mult)
                    V.tensor_tensor(a4[:, :, 0:64], x2, sn, ALU.mult)
                    V.tensor_tensor(a4[:, :, 64:128], x1, sn, ALU.mult).then_inc(free[b], 1)
                    fence()
                    V.tensor_tensor(r4[:, :, 0:64], r4[:, :, 0:64], a4[:, :, 0:64], ALU.subtract)
                    V.tensor_tensor(r4[:, :, 64:128], r4[:, :, 64:128], a4[:, :, 64:128], ALU.add)
                    fence().then_inc(s_rot, 1)
                elif kind == "score":
                    h, m = arg
                    if m == 0:
                        dve.wait_ge(s_strip, h + 1)
                    c0 = SEQ - P - m * P
                    V.scalar_tensor_tensor(prob[h % 2][:, m, :], bank, SCALE, strip[:, h, c0:c0 + SEQ],
                                           ALU.mult, ALU.mult).then_inc(free[b], 1)
                    fence().then_inc(s_prob, 1)
                elif kind == "read":
                    h = arg[0]
                    o = rnorm[:, h, :].rearrange("p (c n) -> p c n", c=NT)
                    for c in range(NT):
                        V.bn_stats(st[:, c, :], bank4[:, c, :])
                    fence()
                    for c in range(NT):
                        V.bn_aggr(mv[:, c, :], st[:, c, :])
                    r = rstd(mv[:, :, 1], NT)
                    for c in range(NT):
                        last = V.tensor_scalar(o[:, c, :], bank4[:, c, :], mv[:, c, 0:1], r[:, c:c + 1],
                                               ALU.subtract, ALU.mult)
                    last.then_inc(free[b], 1)
                    fence().then_inc(s_norm, 1)
                elif kind == "out":
                    t, half = arg
                    z = xh[:, t * D + half * 512:t * D + half * 512 + 512]
                    V.scalar_tensor_tensor(z, z, ALPHA, bank, ALU.mult, ALU.add).then_inc(free[b], 1)
                    if half == 1:
                        if t == 0:
                            dve.wait_ge(s_ln, 32)
                        fence()
                        layer_norm(xh[:, t * D:(t + 1) * D], lnp[:, 0, :], lnp[:, 1, :]).then_inc(s_h, 1)

            def top16(src, values, index, spare):
                V.max(values[:, 0:8], src)
                fence()
                V.max_index(index[:, 0:8], values[:, 0:8], src)
                V.match_replace(spare, values[:, 0:8], src, NEG)
                fence()
                V.max(values[:, 8:16], spare)
                fence()
                V.max_index(index[:, 8:16], values[:, 8:16], spare)

            def choose(u, k):
                V.tensor_copy(sc[:, 0, :], S[:, bass.ts(u, 256)])
                fence()
                for p in range(2):
                    top16(sc[:, 0, p * NK:(p + 1) * NK], top[:, p, :], topi[:, p, :],
                          sc[:, 1, p * NK:(p + 1) * NK])
                fence()
                V.tensor_copy(topf[:], topi[:])
                a = top[:, 0, :].unsqueeze(2).broadcast_to([P, TOPK, TOPK])
                bb = top[:, 1, :].unsqueeze(1).broadcast_to([P, TOPK, TOPK])
                V.tensor_tensor(cand[:].rearrange("p (a b) -> p a b", a=TOPK), a, bb, ALU.add)
                fence()
                top16(cand[:], best[:, k, :], pos[:], sc[:, 0, :])
                fence()
                V.tensor_scalar(posab[:, 0, :], pos[:], 4, None, ALU.logical_shift_right)
                V.tensor_scalar(posab[:, 1, :], pos[:], 15, None, ALU.bitwise_and)
                V.tensor_scalar(negmax[:, k:k + 1], best[:, k, 0:1], -1.0, None, ALU.mult).then_inc(s_best, 1)
                fence()
                V.tensor_copy(posf[:], posab[:])
                fence()
                for p in range(2):
                    e3 = eq[:, p * 256:(p + 1) * 256].rearrange("p (k a) -> p k a", a=TOPK)
                    V.tensor_tensor(e3, posf[:, p, :].unsqueeze(2).broadcast_to([P, TOPK, TOPK]),
                                    iota16[:].unsqueeze(1).broadcast_to([P, TOPK, TOPK]), ALU.is_equal)
                fence()
                for p in range(2):
                    e3 = eq[:, p * 256:(p + 1) * 256].rearrange("p (k a) -> p k a", a=TOPK)
                    V.tensor_tensor(e3, e3, topf[:, p, :].unsqueeze(1).broadcast_to([P, TOPK, TOPK]), ALU.mult)
                fence()
                V.tensor_reduce(pick[:], eq.rearrange("p (q k a) -> p q k a", q=2, a=TOPK), AX.X, ALU.add)
                fence()
                V.scalar_tensor_tensor(idxu[:, k, :], pick[:, 0, :], float(NK), pick[:, 1, :],
                                       ALU.mult, ALU.add).then_inc(s_idxu, 1)
                fence()

            def add_unit(u, k, tile):
                dve.wait_ge(s_vexp, 16 * u + 16)
                yt = y[:, bass.ts(tile, D)]
                V.tensor_tensor(yt, yt, acc[k], ALU.add).then_inc(s_yadd, 1)

            def unit(u, k, tile, before=None, new_tile=False, heads=None):
                if new_tile:
                    V.tensor_copy(hcur, xh[:, bass.ts(tile, D)])
                    fence()

                def products(e0, e1):
                    for e in range(e0, e1):
                        dve.wait_ge(s_u[e % RING], 32 * u + 16 * (1 + e // RING))
                        V.tensor_tensor_reduce(out=urow[e % RING], in0=urow[e % RING], in1=hcur, scale=1.0,
                                               scalar=0.0, op0=ALU.mult, op1=ALU.add,
                                               accum_out=dots[:, k, e:e + 1]).then_inc(s_dot, 1)

                products(0, TOPK // 2)
                if before is not None:
                    add_unit(u - 2, k, before)
                V.tensor_copy(idxv[:, k, :], idxu[:, k, :]).then_inc(s_idxv, 1)
                if heads is not None:
                    dve.wait_ge(s_sc, heads)
                choose(u + 1, 1 - k)
                products(TOPK // 2, TOPK)
                dve.wait_ge(s_exp, u + 1)
                V.reciprocal(rsum[:, k:k + 1], esum[:, k:k + 1])
                fence()
                dve.wait_ge(s_gel, u + 1)
                V.scalar_tensor_tensor(wgt[:, k, :], gel[:, k, :], rsum[:, k:k + 1], eg[:, k, :],
                                       ALU.mult, ALU.mult).then_inc(s_wgt, 1)

            def finish_tile(tile):
                layer_norm(y[:, bass.ts(tile, D)], lnp[:, 0, :], lnp[:, 1, :]).then_inc(s_ln2, 1)
                fence()

            dve.wait_ge(s_sc, 2)
            choose(0, 0)
            dve.wait_ge(s_y, NT)
            dve.wait_ge(s_const, 5)
            for u in range(PH):
                unit(u, u % 2, 0, before=0 if u >= 2 else None, new_tile=u == 0,
                     heads=min(2 * u + 4, 2 * PH))
            dve.wait_ge(s_ln, 64)
            with dve.Fori(1, NT) as tile:
                unit(tile * PH, 0, tile, before=tile - 1, new_tile=True)
                unit(tile * PH + 1, 1, tile, before=tile - 1)
                finish_tile(tile - 1)
                with dve.Fori(1, PH // 2) as j:
                    unit(tile * PH + 2 * j, 0, tile, before=tile)
                    unit(tile * PH + 2 * j + 1, 1, tile, before=tile)
            add_unit(UNITS - 2, 0, NT - 1)
            fence()
            add_unit(UNITS - 1, 1, NT - 1)
            fence()
            finish_tile(NT - 1)

        @block.tensor
        def _(pe):
            T = nc.tensor

            def group(g):
                pe.wait_ge(s_w[g % WRING], 16 * (g // WRING + 1))
                return wring[:, g % WRING, :, :]

            def product(dst, lhs, rhs, n):
                for i in range(n):
                    last = T.matmul(dst, lhs(i), rhs(i), start=(i == 0), stop=(i == n - 1))
                return last

            pe.wait_ge(s_const, 5)
            for kind, arg, by, b, n in JOBS:
                if n:
                    pe.wait_ge(free[b], n)
                bank = ps[:, b, :]
                bank4 = bank.rearrange("p (c n) -> p c n", c=4)
                used = None
                if kind == "xT":
                    t, half = arg
                    if half == 0:
                        pe.wait_ge(s_x[t], 16)
                    for i in range(4):
                        k = 4 * half + i
                        last = T.transpose(bank4[:, i, :], xh[:, t * D + k * P:t * D + (k + 1) * P], ident[:])
                elif kind == "gv":
                    t = arg[0]
                    if t == 0:
                        pe.wait_ge(s_xT, 2 * NT)
                    w = group(GV)
                    last = product(bank, lambda k: xT[:, k, t * P:(t + 1) * P], lambda k: w[:, k, :], KC)
                    used = t == NT - 1
                elif kind == "wsT":
                    pe.wait_ge(s_ws, 16)
                    for h in range(HEADS):
                        last = T.transpose(bank4[:, h, :], ws_raw[:, h, :], ident[:])
                elif kind == "keysT":
                    if arg[0] == 0:
                        pe.wait_ge(s_keys, 16)
                    for i in range(4):
                        last = T.transpose(bank4[:, i, :], keys_raw[:, 4 * arg[0] + i, :], ident[:])
                elif kind == "gu":
                    c = arg[0]
                    w = group(GU)
                    last = product(bank, lambda k: w[:, k, c * P:(c + 1) * P], lambda k: xT[:, k, :], KC)
                    used = c == 3
                elif kind == "mix":
                    h = arg[0]
                    if h == 0:
                        pe.wait_ge(s_vln, NT)
                        pe.wait_ge(s_wsT, 1)
                    for c in range(NT):
                        last = T.matmul(bank4[:, c, :], vln[:, c, h * P:(h + 1) * P], wsT[:, h, :],
                                        start=True, stop=True)
                elif kind == "qk":
                    w_, t = arg
                    w = group(GQ + w_)
                    last = product(bank, lambda k: xT[:, k, t * P:(t + 1) * P], lambda k: w[:, k, :], KC)
                    used = t == NT - 1
                elif kind == "qkT":
                    w_, t = arg
                    pe.wait_ge(s_rot, NT * w_ + t + 1)
                    for h in range(HEADS):
                        last = T.transpose(bank4[:, h, :], tmp[:, t % 2, h * P:(h + 1) * P], ident[:])
                elif kind in ("rv", "rg"):
                    t = arg[0]
                    w = group(GRV if kind == "rv" else GG)
                    last = product(bank, lambda k: xT[:, k, t * P:(t + 1) * P], lambda k: w[:, k, :], KC)
                    used = t == NT - 1
                elif kind == "score":
                    h, m = arg
                    if h == 0 and m == 0:
                        pe.wait_ge(s_qkT, 2 * NT)
                    last = T.matmul(bank, qkT[:, 1, h, m * P:(m + 1) * P], qkT[:, 0, h, :], start=True, stop=True)
                elif kind == "read":
                    h = arg[0]
                    if h == 0:
                        pe.wait_ge(s_rv, NT)
                    pe.wait_ge(s_prob, NT * (h + 1))
                    for c in range(NT):
                        last = product(bank4[:, c, :], lambda m: prob[h % 2][:, m, c * P:(c + 1) * P],
                                       lambda m: rv[:, m, h * P:(h + 1) * P], NT)
                elif kind == "rT":
                    h = arg[0]
                    pe.wait_ge(s_rn, h + 1)
                    for c in range(NT):
                        last = T.transpose(bank4[:, c, :], rnorm[:, h, c * P:(c + 1) * P], ident[:])
                elif kind == "out":
                    t, half = arg
                    if t == 0 and half == 0:
                        pe.wait_ge(s_mix, HEADS)
                        pe.wait_ge(s_rT, HEADS)
                    w = group(GO0 + half)
                    last = product(bank, lambda k: mixT[:, k, t * P:(t + 1) * P], lambda k: w[:, k, :], KC)
                elif kind == "hT":
                    t, half = arg
                    if half == 0:
                        pe.wait_ge(s_h, t + 1)
                    for i in range(4):
                        k = 4 * half + i
                        last = T.transpose(bank4[:, i, :], xh[:, t * D + k * P:t * D + (k + 1) * P], ident[:])
                last.then_inc(full[b], 1)
                if used:
                    T.drain().then_inc(s_wdone, 1)
                if kind == "out" and arg == (NT - 1, 1):
                    T.drain().then_inc(s_wdone, 2)
                if kind == "score" and arg == (HEADS - 1, NT - 1):
                    T.drain().then_inc(s_scored, 1)

            def head(h):
                for kind, (_, p), _, b, n in HJOBS[h]:
                    pe.wait_ge(free[b], n)
                    if kind == "query":
                        if p == 0:
                            pe.wait_ge(s_wq[h % 2], 16 * (h // 2 + 1))
                            if h == 0:
                                pe.wait_ge(s_hT, 2 * NT)
                        last = product(ps[:, b, :], lambda k: wq[:, h % 2, k, p * P:(p + 1) * P],
                                       lambda k: xT[:, k, :], KC)
                        last.then_inc(full[b], 1)
                        if p == 1:
                            T.drain().then_inc(s_wqd, 1)
                    else:
                        pe.wait_ge(s_qh, 2 * h + p + 1)
                        if h == 0 and p == 0:
                            pe.wait_ge(s_keysT, 4)
                        for t in range(NT):
                            last = T.matmul(ps[:, b, t * P:(t + 1) * P], qh[:, h % 2, p, t * P:(t + 1) * P],
                                            keysT[:, 2 * h + p, :], start=True, stop=True)
                        last.then_inc(full[b], 1)

            def unit(u, k, first):
                if not first:
                    pe.wait_ge(s_yadd, u - 1)
                for e in range(TOPK):
                    pe.wait_ge(s_v[e % RING], 32 * u + 16 * (1 + e // RING))
                    pe.wait_ge(s_diag, 16 * u + e + 1)
                    for half in range(2):
                        last = T.matmul(acc[k][:, half * 512:(half + 1) * 512], diag[:, e % NDIAG, :],
                                        vrow[e % RING][:, half * 512:(half + 1) * 512],
                                        start=(e == 0), stop=(e == TOPK - 1))
                    last.then_inc(s_vexp, 1)

            for h in range(3):
                head(h)
            for b in range(4):
                pe.wait_ge(free[b], USED[b])
            for u in range(6):
                unit(u, u % 2, u < 2)
                if u < 5:
                    head(3 + u)
            with pe.Fori(3, UNITS // 2) as pair:
                unit(2 * pair, 0, False)
                unit(2 * pair + 1, 1, False)


_INS = ["x", "w_in", "sgu_ln_w", "sgu_ln_b", "sgu_w_s", "sgu_b", "ret_decay_fwd", "ret_decay_bwd", "ret_gn_w",
        "w_out", "ln1_w", "ln1_b", "peer_w_q", "peer_sub_keys", "peer_u", "peer_v", "ln2_w", "ln2_b"]


def kernel(**inputs):
    import numpy as _np
    import concourse.bacc as _bacc
    from concourse import mybir as _mybir
    from concourse.bass_utils import run_bass_kernel_spmd as _run

    nc = _bacc.Bacc("TRN2", target_bir_lowering=False, num_devices=1)
    arrays, args = {}, []
    for name in _INS:
        a = _np.ascontiguousarray(inputs[name])
        arrays[f"in_{name}_dram"] = a
        args.append(nc.dram_tensor(f"in_{name}_dram", a.shape, _mybir.dt.from_np(a.dtype), kind="ExternalInput").ap())
    half = P // 2
    inv = _np.float32(10000.0) ** (-_np.arange(half, dtype=_np.float32) / _np.float32(half))
    ang = _np.arange(SEQ, dtype=_np.float32)[:, None] * inv[None, :].astype(_np.float32)
    table = _np.stack([_np.cos(ang), _np.sin(ang)], axis=1).astype(_np.float32)
    table = _np.ascontiguousarray(table.reshape(NT, P, 2, half).transpose(1, 0, 2, 3))
    arrays["rope_dram"] = table
    args.append(nc.dram_tensor("rope_dram", table.shape, _mybir.dt.float32, kind="ExternalInput").ap())
    out = nc.dram_tensor("out_dram", (1, SEQ, D), _mybir.dt.float32, kind="ExternalOutput").ap()
    layer(nc, *args, out)
    r = _run(nc, [arrays], core_ids=[0])
    return r.results[0]["out_dram"]
```

```python
import numpy as np
import concourse.bass as bass
from concourse import mybir
from contextlib import ExitStack

P = 128
SEQ, D = 512, 1024
NT = SEQ // P
KC = D // P
GW = 512
HEADS = 4
PH, TOPK, NK = 8, 16, 128
UNITS = NT * PH
RING = 8
NDIAG = 8
LAST = 12
TILE0 = 4
HEAD_ORDER = list(range(TILE0, PH)) + list(range(TILE0))
EARLY = 7
ALPHA = 2.0 ** 0.25
EPS = 1e-5
SCALE = float(P) ** -0.5
STRIP = 2 * SEQ - P
NEG = -3.0e38
GV, GU, GQ, GK, GRV, GG = range(6)
GROUP_COL = {GV: 512, GU: 0, GQ: 1024, GK: 1536, GRV: 2048, GG: 2560}
WRING = 4
WPART = 4


def static_jobs():
    jobs = []

    def add(kind, *arg, by):
        jobs.append((kind, arg, by))

    def split(g, *parts):
        for c in parts:
            jobs.append(("split", (g, c), None))

    def transposed(t):
        add("xT", t, 0, by="dve")
        add("xT", t, 1, by="dve")

    transposed(0)
    split(GV, 0)
    transposed(1)
    split(GV, 1, 2, 3)
    for t in range(NT):
        add("gv", t, by="act")
        if t + 2 < NT:
            transposed(t + 2)
        if t in (1, 2):
            split(GU, 2 * (t - 1), 2 * (t - 1) + 1)
    add("wsT", by="act")
    for q in range(4):
        add("keysT", q, by="dve")
    for c in range(4):
        add("gu", c, by="act")
        if c < 2:
            split(GQ, 2 * c, 2 * c + 1)
    for h in range(HEADS):
        add("mix", h, by="dve")
    for i in range(2 * NT):
        w, t = divmod(i, NT)
        add("qk", w, t, by="dve")
        if i:
            add("qkT", *divmod(i - 1, NT), by="act")
        if t in (1, 2):
            split(GK + w, 2 * t - 2, 2 * t - 1)
    for t in range(NT):
        add("rv", t, by="act")
        if t == 0:
            add("qkT", 1, NT - 1, by="act")
        if t < 2:
            split(GG, 2 * t, 2 * t + 1)
    def score(h):
        for m in range(NT):
            add("score", h, m, by="dve")

    score(0)
    add("rg", 0, by="act")
    score(1)
    add("rg", 1, by="act")
    add("read", 0, by="dve")
    add("rg", 2, by="act")
    add("rg", 3, by="act")
    score(2)
    add("read", 1, by="dve")
    score(3)
    jobs.append(("norm", (1,), None))
    add("read", 2, by="dve")
    add("read", 3, by="dve")
    jobs.append(("norm", (3,), None))
    add("outA", 0, 0, by="dve")
    add("outA", 0, 1, by="dve")
    for h in range(HEADS):
        add("rT", h, by="act")
    front = len(jobs)
    for kind, *arg in (("out", 0, 0), ("out", 0, 1), ("outA", 1, 0), ("hT", 0, 0), ("hT", 0, 1),
                       ("query0", 0), ("keys0", 0), ("query0", 1), ("keys0", 1), ("outA", 1, 1),
                       ("out", 1, 0), ("out", 1, 1), ("out", 2, 0), ("out", 2, 1), ("query0", 2), ("keys0", 2),
                       ("out", 3, 0), ("out", 3, 1),
                       ("V", 0, 0, 8), ("query0", 3), ("keys0", 3), ("hT", 1, 0), ("hT", 1, 1),
                       ("V", 0, 8, TOPK), ("hT", 2, 0), ("hT", 2, 1)):
        add(kind, *arg, by="dve" if kind in ("out", "outA") else "act")
    for u in range(1, EARLY):
        turns = {5: [4, 5], 6: [6, 7]}.get(u, [u - 1])
        cut = [0, 3, 6, 9, 12, TOPK] if len(turns) == 2 else [0, 6, 11, TOPK]
        parts = [[("query", n, p)] for n in turns for p in range(2)]
        for n, i in zip(turns, (1, 3)):
            parts[i] += [("keys", n, 0), ("keys", n, 1)]
        if u == 1:
            parts[0] = [("hT", 3, 0), ("hT", 3, 1)] + parts[0]
        for i, e in enumerate(cut[:-1]):
            add("V", u, e, cut[i + 1], by="act")
            for kind, *arg in parts[i] if i < len(parts) else []:
                add(kind, *arg, by="act")
    placed, used, n_front, n_score, n_late = [], [0] * 8, 0, 0, 0
    scoring = late = False
    for i, (kind, arg, by) in enumerate(jobs):
        if kind in ("V", "split", "norm"):
            placed.append((kind, arg, by, None, None))
            continue
        if kind == "out" and arg[0] < 2:
            b, n = next((b, n) for k, a, _, b, n in placed if k == "outA" and a == arg)
            placed.append((kind, arg, by, b, n))
            continue
        scoring = scoring or kind == "score"
        b = n_front % 8
        n_front += 1
        late = late or kind == "outA"
        if kind == "outA":
            b = 2 * arg[0] + arg[1]
        elif kind == "read":
            b = 4 + arg[0]
        elif scoring and not late:
            b = n_score % 4
            n_score += 1
        elif late:
            b = 4 + n_late % 4
            n_late += 1
        placed.append((kind, arg, by, b, used[b]))
        used[b] += 1
    return placed, used, front


def layer(nc, x, w_in, sgu_ln_w, sgu_ln_b, sgu_w_s, sgu_b, decay_fwd, decay_bwd, gn_w, w_out, ln1_w, ln1_b,
          w_q, sub_keys, peer_u, peer_v, ln2_w, ln2_b, rope, out):
    f32, i32 = mybir.dt.float32, mybir.dt.int32
    u32 = mybir.dt.uint32
    f32r = mybir.dt.float32r
    ALU, ACT = mybir.AluOpType, mybir.ActivationFunctionType
    AX = mybir.AxisListType

    JOBS, USED, FRONT = static_jobs()
    BANK = {(kind,) + arg: (b, n) for kind, arg, _, b, n in JOBS}

    ctx = ExitStack()
    with ctx:
        def sb(name, shape, dt=f32):
            return ctx.enter_context(nc.sbuf_tensor(name, shape, dt))

        def sem(name):
            return ctx.enter_context(nc.semaphore(name))

        def parts(name, shape):
            with nc.sbuf_tensor(name, shape, f32r) as view:
                return view

        wparts = parts("weight_parts", [P, WRING * KC * GW])[:, :].rearrange("p (s k n) -> p s k n", s=WRING, k=KC)
        big = sb("big", [P, 2 * RING * D])
        wring = big[:, :].rearrange("p (s k n) -> p s k n", s=WRING, k=KC)
        rows = big[:, :].rearrange("p (s n) -> p s n", n=D)
        urow = [rows[:, s, :] for s in range(RING)]
        vrow = [rows[:, RING + s, :] for s in range(RING)]
        xlo = parts("x_lo", [P, NT * D])[:, :].rearrange("p (t k n) -> p t k n", t=NT, k=KC)
        xh = sb("xh", [P, NT * D])
        xhi = parts("x_hi", [P, KC * SEQ])[:, :].rearrange("p (k n) -> p k n", k=KC)
        xT = sb("xT", [P, KC, SEQ])
        def w_lo(g):
            return wparts[:, 2 * (g % 2), :, :]

        def w_hi(g):
            return wparts[:, 2 * (g % 2) + 1, :, :]

        def w_full(g):
            return wring[:, 2 * (g % 2), :, :]

        prob1 = big[:, 0:2048].rearrange("p (m n) -> p m n", m=NT)
        rnorm = big[:, 2048:4096].rearrange("p (h n) -> p h n", h=HEADS)
        y = sb("y", [P, NT * D])
        strip = y[:, 0:HEADS * STRIP].rearrange("p (h n) -> p h n", h=HEADS)
        S = sb("S", [P, UNITS * 256 + 256])
        vrow0 = [S[:, s * D:(s + 1) * D] for s in range(RING)]
        S4 = S[:, 0:UNITS * 256].rearrange("p (t q n) -> p t q n", t=NT, q=2 * PH)
        rv = S[:, 0:2048].rearrange("p (t n) -> p t n", t=NT)
        gate = S[:, 2048:4096].rearrange("p (t n) -> p t n", t=NT)
        keys_raw = S[:, 2048:4096].rearrange("p (q n) -> p q n", q=2 * PH)
        gains = S[:, 4096:6144].rearrange("p (g n) -> p g n", g=4)
        prob0 = S[:, 6144:8192].rearrange("p (m n) -> p m n", m=NT)
        ws_raw = S[:, 6144:6656].rearrange("p (h n) -> p h n", h=HEADS)
        tmp = S[:, 6144:8192].rearrange("p (m n) -> p m n", m=NT)
        prob = [prob0, prob1]
        mixT = sb("mixT", [P, KC, SEQ])
        vln = mixT[:, 4:8, :]
        mix1 = mixT[:, :, :].rearrange("p k n -> p (k n)")
        ahead, behind = (mix1[:, 2048 + 1024 * i:2048 + 1024 * i + STRIP] for i in range(2))
        hcur0, hcur1 = y[:, 0:D], mix1[:, 0:D]
        work0, work1 = y[:, D:2 * D], mix1[:, 3 * D:4 * D]
        qh0 = y[:, 2 * D:2 * D + 512].rearrange("p (s q n) -> p s q n", s=2, q=2)
        qh = mix1[:, D:3 * D].rearrange("p (s q n) -> p s q n", s=2, q=2)
        qkT = sb("qkT", [P, 2, HEADS, SEQ])
        qk1 = qkT[:, :, :, :].rearrange("p a h n -> p (a h n)")
        wq = qk1.rearrange("p (s k n) -> p s k n", s=2, k=KC)
        lnp = sb("lnp", [P, 2, D])
        keysT = sb("keysT", [P, 2 * PH, NK])
        wsT = sb("wsT", [P, HEADS, P])
        ropet = sb("ropet", [P, NT, 2, 64])
        S0 = [m[:, i:i + 256] for m in (ropet[:, :, :, :].rearrange("p t a n -> p (t a n)"),
                                        wsT[:, :, :].rearrange("p h n -> p (h n)")) for i in (0, 256)]
        ident = sb("ident", [P, P])
        diag = sb("diag", [P, NDIAG, P])
        iota16 = sb("iota16", [P, TOPK])
        dec = sb("dec", [P, 10, 2 * HEADS])
        st = sb("st", [P, 8, 6])
        mv = sb("mv", [P, 8, 2])
        nw = sb("nw", [P, 4, 8])
        top = sb("top", [P, 2, TOPK])
        topi = sb("topi", [P, 2, TOPK], u32)
        topf = sb("topf", [P, 2, TOPK])
        best = sb("best", [P, 2, TOPK])
        pos = sb("pos", [P, TOPK], u32)
        posab = sb("posab", [P, 2, TOPK], u32)
        posf = sb("posf", [P, 2, TOPK])
        pick = sb("pick", [P, 2, TOPK])
        idxu = sb("idxu", [P, 2, TOPK], i32)
        idxv = sb("idxv", [P, 2, TOPK], i32)
        negmax = sb("negmax", [P, 2])
        esum = sb("esum", [P, 2])
        rsum = sb("rsum", [P, 2])
        eg = sb("eg", [P, 2, TOPK])
        dots = sb("dots", [P, 2, TOPK])
        gel = sb("gel", [P, 2, TOPK])
        wgt = sb("wgt", [P, 2, TOPK])
        ps = ctx.enter_context(nc.psum_tensor("ps", [P, 8, 512], f32))
        acc = [ps[:, 2 * k:2 * k + 2, :].rearrange("p a n -> p (a n)") for k in range(2)]

        full = [sem(f"bank_full{b}") for b in range(8)]
        free = [sem(f"bank_free{b}") for b in range(8)]
        s_x = [sem(f"x_loaded{t}") for t in range(NT)]
        s_w = [[sem(f"weights_loaded{s}_{c}") for c in range(WPART)] for s in range(2)]
        s_whi, s_gvlo, s_wlo = sem("weights_hi_ready"), sem("weights_gv_lo_ready"), sem("weights_lo_ready")
        s_wo = [sem(f"w_out_loaded{s}") for s in range(2)]
        s_wdone = sem("weights_used")
        s_ws, s_keys, s_rope = sem("ws_loaded"), sem("keys_loaded"), sem("rope_loaded")
        s_gain, s_dec, s_ln = sem("gains_loaded"), sem("decay_loaded"), sem("ln_loaded")
        s_const = sem("constants_ready")
        s_xhi, s_xT = sem("xT_hi_ready"), sem("xT_ready")
        s_wsT, s_keysT = sem("wsT_ready"), sem("keysT_ready")
        s_gv, s_vln = sem("gelu_v_ready"), sem("vln_ready")
        s_gu, s_mix = sem("gelu_u_ready"), sem("gating_ready")
        s_adec, s_edec = sem("absdecay_ready"), sem("expdecay_ready")
        s_z, s_strip = sem("logstrip_ready"), sem("strip_ready")
        s_rot, s_qkT = sem("rotated_ready"), sem("qkT_ready")
        s_rv, s_gate = sem("rv_ready"), sem("gate_ready")
        s_scored = sem("scores_done")
        s_norm = sem("normalised_ready")
        s_gg = sem("gate_times_gain_ready")
        s_prob, s_rn, s_rT = sem("prob_ready"), sem("retention_ready"), sem("retentionT_ready")
        s_h, s_hT, s_y = sem("h_ready"), sem("hT_ready"), sem("y_started")
        s_wq = [sem(f"wq_loaded{s}") for s in range(2)]
        s_wqd = sem("wq_used")
        s_qh, s_sc = sem("query_ready"), sem("key_scores_ready")
        s_qh0, s_sc0 = sem("query0_ready"), sem("key_scores0_ready")
        s_best, s_exp = sem("best_ready"), sem("exp_ready")
        s_idxu, s_idxv = sem("indices_u_ready"), sem("indices_v_ready")
        s_u = [sem(f"urow_gathered{s}") for s in range(RING)]
        s_v = [sem(f"vrow_gathered{s}") for s in range(RING)]
        s_dot, s_gel, s_wgt = sem("dots_done"), sem("gelu_ready"), sem("expert_weights_ready")
        s_diag, s_vexp = sem("diag_ready"), sem("experts_added")
        s_yadd = sem("unit_added")
        s_ln2, s_out = sem("output_ready"), sem("output_stored")

        peer_u2, peer_v2 = peer_u[0], peer_v[0]
        w_in3 = w_in[0].rearrange("(k p) n -> p k n", p=P)
        w_out3 = w_out[0].rearrange("(k p) n -> p k n", p=P)
        w_q3 = w_q[0].rearrange("(k p) n -> p k n", p=P)
        out3 = out[0].rearrange("(t p) n -> p t n", p=P)

        def w_low(engine, g, c):
            ks = slice(c * KC // WPART, (c + 1) * KC // WPART)
            return engine.tensor_tensor(w_lo(g)[:, ks, :], w_full(g)[:, ks, :], w_hi(g)[:, ks, :].bitcast(f32),
                                        ALU.subtract)

        block = ctx.enter_context(nc.Block())

        @block.sync
        def _(sp):
            def load_group(g, parts=range(WPART)):
                if g >= 2:
                    sp.wait_ge(s_wdone, g - 1)
                c0, n = GROUP_COL[g], KC // WPART
                for c in parts:
                    sp.dma_start(w_full(g)[:, c * n:(c + 1) * n, :], w_in3[:, c * n:(c + 1) * n, c0:c0 + GW]
                                 ).then_inc(s_w[g % 2][c], 16)

            def load_x(t):
                sp.dma_start(xh[:, t * D:(t + 1) * D], x[0, t * P:(t + 1) * P, :]).then_inc(s_x[t], 16)

            load_x(0)
            load_group(GV, (0,))
            load_x(1)
            load_group(GV, (1, 2, 3))
            sp.dma_start(dec[:, 0, 0:HEADS], decay_fwd[0].partition_broadcast(P)).then_inc(s_dec, 16)
            sp.dma_start(dec[:, 0, HEADS:], decay_bwd[0].partition_broadcast(P)).then_inc(s_dec, 16)
            for t in range(2, NT):
                load_x(t)
            for i, row in enumerate((sgu_ln_w[0], sgu_ln_b[0], gn_w[0], sgu_b[0].rearrange("h l -> (h l)"))):
                sp.dma_start(gains[:, i, :], row.partition_broadcast(P)).then_inc(s_gain, 16)
            load_group(GU)
            sp.dma_start(ws_raw, sgu_w_s[0].rearrange("h l m -> l h m")).then_inc(s_ws, 16)
            sp.dma_start(keys_raw, sub_keys[0].rearrange("h q n d -> n (h q) d")).then_inc(s_keys, 16)
            load_group(GQ)
            sp.dma_start(ropet[:], rope).then_inc(s_rope, 16)
            load_group(GK)
            sp.dma_start(lnp[:, 0, :], ln1_w[0].partition_broadcast(P)).then_inc(s_ln, 16)
            sp.dma_start(lnp[:, 1, :], ln1_b[0].partition_broadcast(P)).then_inc(s_ln, 16)
            load_group(GRV)
            load_group(GG)
            sp.wait_ge(s_wdone, 6)
            for half in range(2):
                sp.dma_start(wring[:, 2 + half, :, :], w_out3[:, :, half * GW:(half + 1) * GW]
                             ).then_inc(s_wo[half], 16)
            for t in range(NT):
                load_x(t)
            sp.wait_ge(s_scored, 1)
            for n, h in enumerate(list(range(TILE0)) + HEAD_ORDER):
                if n >= 2:
                    sp.wait_ge(s_wqd, n - 1)
                sp.dma_start(wq[:, n % 2, :, :], w_q3[:, :, h * 256:(h + 1) * 256]).then_inc(s_wq[n % 2], 16)
                if n == TILE0:
                    sp.wait_ge(s_h, 2 * NT)
                    sp.dma_start(lnp[:, 0, :], ln2_w[0].partition_broadcast(P)).then_inc(s_ln, 16)
                    sp.dma_start(lnp[:, 1, :], ln2_b[0].partition_broadcast(P)).then_inc(s_ln, 16)
            for t in range(NT):
                for half in range(2):
                    sp.wait_ge(s_ln2, 2 * t + half + 1)
                    c = half * 512
                    sp.dma_start(out3[:, t, c:c + 512], y[:, t * D + c:t * D + c + 512]).then_inc(s_out, 16)
            sp.wait_ge(s_out, 32 * NT)

        @block.gpsimd
        def _(pool):
            nc.gpsimd.memset(ident[:], 0.0).then_inc(s_const, 1)
            nc.gpsimd.memset(S[:, UNITS * 256:], 0.0).then_inc(s_const, 1)
            nc.gpsimd.iota(iota16[:], pattern=[[1, TOPK]], base=0, channel_multiplier=0,
                           allow_small_or_imprecise_dtypes=True).then_inc(s_const, 1)
            pool.wait_ge(s_const, 3)
            nc.gpsimd.affine_select(out=ident[:], in_=ident[:], compare_op=ALU.not_equal, fill=1.0, base=0,
                                    pattern=[[-1, P]], channel_multiplier=1).then_inc(s_const, 1)
            for g in range(GU, GG + 1):
                for c in range(WPART):
                    pool.wait_ge(s_whi, WPART * g + c + 1)
                    w_low(nc.gpsimd, g, c).then_inc(s_wlo, 1)
                if g == GK:
                    pool.wait_ge(s_mix, HEADS)
                    nc.gpsimd.iota(ahead, pattern=[[1, STRIP]], base=-(SEQ - P), channel_multiplier=-1,
                                   allow_small_or_imprecise_dtypes=True).then_inc(s_const, 1)
            pool.wait_ge(s_gain, 64)
            for t in range(NT):
                pool.wait_ge(s_gate, t + 1)
                nc.gpsimd.tensor_tensor(gate[:, t, :], gate[:, t, :], gains[:, 2, :], ALU.mult).then_inc(s_gg, 1)
            pool.wait_ge(s_gg, NT)
            for h in range(HEADS):
                pool.wait_ge(s_norm, h + 1)
                o = rnorm[:, h, :].rearrange("p (c n) -> p c n", c=NT)
                nc.gpsimd.tensor_tensor(o, o, gate[:, :, h * P:(h + 1) * P], ALU.mult).then_inc(s_rn, 1)
            pool.wait_ge(s_rT, HEADS)

            def gather(table, row, index, e, signal):
                nc.gpsimd.indirect_dma_start(row[e % RING], None, table,
                                             bass.IndirectOffsetOnAxis(ap=index[:, e:e + 1], axis=0)
                                             ).then_inc(signal[e % RING], 16)

            def block_of_gathers(u, k, last=False):
                pool.wait_ge(s_idxv, u + 1)
                pool.nop(nofuse=True)
                if not last:
                    pool.wait_ge(s_idxu, u + 2)
                    pool.nop(nofuse=True)
                step = 2 if last else 4
                for e in range(TOPK):
                    if e % step == 0:
                        pool.wait_ge(s_vexp, 16 * u + e + step - RING)
                        pool.nop(nofuse=True)
                    gather(peer_v2, vrow, idxv[:, k, :], e, s_v)
                    if not last:
                        if e % 4 == 0:
                            pool.wait_ge(s_dot, 16 * u + 16 + e + 4 - RING)
                            pool.nop(nofuse=True)
                        gather(peer_u2, urow, idxu[:, 1 - k, :], e, s_u)

            def gathers(table, row, index, signal, e0, e1):
                for e in range(e0, e1):
                    gather(table, row, index, e, signal)

            pool.wait_ge(s_idxu, 1)
            gathers(peer_u2, urow, idxu[:, 0, :], s_u, 0, RING)
            pool.wait_ge(s_idxv, 1)
            gathers(peer_v2, vrow0, idxv[:, 0, :], s_v, 0, 4)
            for e in (0, 4):
                pool.wait_ge(s_dot, e + 4)
                gathers(peer_u2, urow, idxu[:, 0, :], s_u, RING + e, RING + e + 4)
            gathers(peer_v2, vrow0, idxv[:, 0, :], s_v, 4, RING)
            pool.wait_ge(s_idxu, 2)
            for e in (0, 4):
                pool.wait_ge(s_dot, RING + e + 4)
                gathers(peer_u2, urow, idxu[:, 1, :], s_u, e, e + 4)
            for e in (RING, RING + 4):
                pool.wait_ge(s_vexp, e + 4 - RING)
                gathers(peer_v2, vrow0, idxv[:, 0, :], s_v, e, e + 4)
                pool.wait_ge(s_dot, 16 + e + 4 - RING)
                gathers(peer_u2, urow, idxu[:, 1, :], s_u, e, e + 4)
            pool.wait_ge(s_wdone, 8)
            block_of_gathers(1, 1)
            with pool.Fori(1, UNITS // 2 - 1) as pair:
                block_of_gathers(2 * pair, 0)
                block_of_gathers(2 * pair + 1, 1)
            block_of_gathers(UNITS - 2, 0)
            block_of_gathers(UNITS - 1, 1, last=True)

        @block.scalar
        def _(act):
            A = nc.scalar

            def copy(dst, src):
                return A.activation(dst, src, ACT.Copy)

            def exps(u, k):
                act.wait_ge(s_best, u + 1)
                A.activation(eg[:, k, :], best[:, k, :], ACT.Exp, bias=negmax[:, k:k + 1],
                             accum_out=esum[:, k:k + 1]).then_inc(s_exp, 1)

            def begin_unit(u, k):
                exps(u + 1, 1 - k)
                act.wait_ge(s_dot, 16 * u + 16)
                A.activation(gel[:, k, :], dots[:, k, :], ACT.Gelu).then_inc(s_gel, 1)
                act.wait_ge(s_wgt, u + 1)

            def diagonals(u, k, e0=0, e1=TOPK, first=False):
                for e in range(e0, e1):
                    if (e % 4 == 0 or e == e0) and not (first and e < NDIAG):
                        act.wait_ge(s_vexp, 16 * u + min(e - e % 4 + 4, e1) - NDIAG)
                    A.activation(diag[:, e % NDIAG, :], ident[:], ACT.Copy,
                                 scale=wgt[:, k, e:e + 1]).then_inc(s_diag, 1)

            act.wait_ge(s_const, 4)
            A.activation(gel[:, 0, 0:1], ident[:, 0:1], ACT.Gelu)
            for kind, arg, by, b, n in JOBS:
                if kind == "V":
                    u, e0, e1 = arg
                    if e0 == 0:
                        begin_unit(u, u % 2)
                        written = 0
                    upto = min(e1 + 2, TOPK)
                    diagonals(u, u % 2, written, upto, first=u == 0)
                    written = upto
                    if u == 1 and e0 < 11:
                        for t in range(0, 1) if e0 == 0 else range(1, NT):
                            A.activation(y[:, t * D:(t + 1) * D], xh[:, t * D:(t + 1) * D], ACT.Copy,
                                         scale=ALPHA).then_inc(s_y, 1)
                    continue
                if kind == "split":
                    g, c = arg
                    ks = slice(c * KC // WPART, (c + 1) * KC // WPART)
                    act.wait_ge(s_w[g % 2][c], 16 * (g // 2 + 1))
                    copy(w_hi(g)[:, ks, :], w_full(g)[:, ks, :]).then_inc(s_whi, 1)
                    continue
                if by != "act" and kind != "xT":
                    continue
                act.wait_ge(full[b], n + 1)
                bank = ps[:, b, :]
                bank4 = bank.rearrange("p (c n) -> p c n", c=4)
                if kind == "xT":
                    t, half = arg
                    copy(xhi[:, 4 * half:4 * half + 4, t * P:(t + 1) * P], bank4).then_inc(s_xhi, 1)
                elif kind == "gv":
                    A.activation(vln[:, arg[0], :], bank, ACT.Gelu).then_inc(free[b], 1)
                    A.drain().then_inc(s_gv, 1)
                elif kind == "wsT":
                    copy(wsT[:], bank4).then_inc(free[b], 1)
                    A.drain().then_inc(s_wsT, 1)
                elif kind == "gu":
                    A.activation(mixT[:, arg[0], :], bank, ACT.Gelu).then_inc(free[b], 1)
                    A.drain().then_inc(s_gu, 1)
                    if arg[0] == 3:
                        act.wait_ge(s_adec, 1)
                        A.activation(dec[:, 3, :], dec[:, 2, :], ACT.Exp, scale=-1.0).then_inc(s_edec, 1)
                elif kind == "qkT":
                    w, t = arg
                    copy(qkT[:, w, :, t * P:(t + 1) * P], bank4).then_inc(free[b], 1)
                    A.drain().then_inc(s_qkT, 1)
                elif kind == "rv":
                    copy(rv[:, arg[0], :], bank).then_inc(free[b], 1)
                    A.drain().then_inc(s_rv, 1)
                    if arg[0] == 3:
                        for h in range(HEADS):
                            act.wait_ge(s_z, h + 1)
                            A.activation(strip[:, h, :], strip[:, h, :], ACT.Exp).then_inc(s_strip, 1)
                elif kind == "rg":
                    A.activation(gate[:, arg[0], :], bank, ACT.Silu).then_inc(free[b], 1)
                    A.drain().then_inc(s_gate, 1)
                elif kind == "rT":
                    copy(mixT[:, 4 + arg[0], :], bank).then_inc(free[b], 1)
                    A.drain().then_inc(s_rT, 1)
                elif kind == "hT":
                    t, half = arg
                    copy(xT[:, 4 * half:4 * half + 4, t * P:(t + 1) * P], bank4).then_inc(free[b], 1)
                    A.drain().then_inc(s_hT, 1)
                elif kind == "query0":
                    h = arg[0]
                    copy(qh0[:, h % 2, :, :], bank4[:, 0:2, :]).then_inc(free[b], 1)
                    A.drain().then_inc(s_qh0, 1)
                elif kind == "keys0":
                    h = arg[0]
                    copy(S0[h], bank[:, 0:256]).then_inc(free[b], 1)
                    A.drain().then_inc(s_sc0, 1)
                    if h == 0:
                        exps(0, 0)
                elif kind == "query":
                    n_, p = arg
                    t0 = 0 if HEAD_ORDER[n_] >= TILE0 else 1
                    copy(qh[:, n_ % 2, p, t0 * P:], bank[:, t0 * P:]).then_inc(free[b], 1)
                    A.drain().then_inc(s_qh, 1)
                elif kind == "keys":
                    n_, p = arg
                    h = HEAD_ORDER[n_]
                    t0 = 0 if h >= TILE0 else 1
                    copy(S4[:, t0:, 2 * h + p, :], bank4[:, t0:, :]).then_inc(free[b], 1)
                    A.drain().then_inc(s_sc, 1)

            for u in range(EARLY, PH):
                begin_unit(u, u % 2)
                diagonals(u, u % 2)
            with act.Fori(PH // 2, UNITS // 2 - 1) as pair:
                for k in range(2):
                    begin_unit(2 * pair + k, k)
                    diagonals(2 * pair + k, k)
            begin_unit(UNITS - 2, 0)
            diagonals(UNITS - 2, 0)
            begin_unit(UNITS - 1, 1)
            diagonals(UNITS - 1, 1, 0, LAST)

        @block.vector
        def _(dve):
            V = nc.vector
            fence = V.drain

            def rstd(var, n, post=None):
                v, r, a = nw[:, 0, 0:n], nw[:, 3, 0:n], nw[:, 1, 0:n]
                if n == 1:
                    neg_half = st[:, 7, 0:1]
                half = nw[:, 2, 0:n].bitcast(i32)
                fence()
                V.tensor_scalar(v, var, EPS, None, ALU.add)
                fence()
                V.tensor_scalar(half, v.bitcast(i32), 1, None, ALU.logical_shift_right)
                if n == 1:
                    V.tensor_scalar(neg_half, v, -0.5, None, ALU.mult)
                fence()
                V.tensor_scalar(r.bitcast(i32), half, -1.0, float(0x5F3759DF), ALU.mult, ALU.add)
                for _ in range(3):
                    fence()
                    if n == 1:
                        V.scalar_tensor_tensor(a, r, neg_half, r, ALU.mult, ALU.mult)
                    else:
                        V.tensor_tensor(a, r, r, ALU.mult)
                        fence()
                        V.scalar_tensor_tensor(a, a, -0.5, v, ALU.mult, ALU.mult)
                    fence()
                    V.scalar_tensor_tensor(r, a, 1.5, r, ALU.add, ALU.mult)
                fence()
                return r

            def layer_norm(z, w, b, done=None, known=0):
                width = z.shape[-1]
                n = width // 512
                for i in range(known, n):
                    V.bn_stats(st[:, i, :], z[:, i * 512:(i + 1) * 512])
                fence()
                V.bn_aggr(mv[:, 0, :], st[:, 0:n, :].rearrange("p a b -> p (a b)"))
                r = rstd(mv[:, 0, 1:2], 1)
                for i in range(n):
                    c = slice(i * 512, (i + 1) * 512)
                    V.scalar_tensor_tensor(z[:, c], z[:, c], mv[:, 0, 0:1], w[:, c], ALU.subtract, ALU.mult)
                    fence()
                    last = V.scalar_tensor_tensor(z[:, c], z[:, c], r, b[:, c], ALU.mult, ALU.add)
                    if done is not None and i < n - 1:
                        last.then_inc(done, 1)
                return last

            def decay_strips():
                x0, neg, ab, e, z, z2, p, lo = (dec[:, i, :] for i in range(8))
                lg = dec[:, 8, :]
                den = dec[:, 9, :]
                dve.wait_ge(s_edec, 1)
                V.tensor_scalar(den, e, 2.0, None, ALU.add)
                fence()
                V.reciprocal(den, den)
                fence()
                V.tensor_tensor(z, e, den, ALU.mult)
                fence()
                V.tensor_tensor(z2, z, z, ALU.mult)
                fence()
                V.tensor_scalar(p, z2, 1.0 / 17, None, ALU.mult)
                for k in range(15, 1, -2):
                    fence()
                    V.scalar_tensor_tensor(p, p, 1.0 / k, z2, ALU.add, ALU.mult)
                V.tensor_scalar(lo, x0, 0.0, None, ALU.min)
                fence()
                V.scalar_tensor_tensor(p, p, 1.0, z, ALU.add, ALU.mult)
                fence()
                V.scalar_tensor_tensor(lg, p, -2.0, lo, ALU.mult, ALU.add)
                dve.wait_ge(s_const, 5)
                V.tensor_scalar(behind, ahead, -1.0, 0.0, ALU.mult, ALU.max)
                fence()
                V.tensor_scalar(ahead, ahead, 0.0, None, ALU.max)
                fence()
                for h in range(HEADS):
                    V.tensor_scalar(strip[:, h, :], behind, lg[:, HEADS + h:HEADS + h + 1], None, ALU.mult)
                    fence()
                    V.scalar_tensor_tensor(strip[:, h, :], ahead, lg[:, h:h + 1], strip[:, h, :],
                                           ALU.mult, ALU.add).then_inc(s_z, 1)
                    fence()

            cos = ropet[:, :, 0, :]
            sin = ropet[:, :, 1, :]
            for kind, arg, by, b, n in JOBS[:FRONT]:
                if kind == "wsT":
                    dve.wait_ge(s_dec, 32)
                    V.tensor_scalar(dec[:, 1, :], dec[:, 0, :], -1.0, None, ALU.mult)
                    fence()
                    V.tensor_tensor(dec[:, 2, :], dec[:, 0, :], dec[:, 1, :], ALU.max).then_inc(s_adec, 1)
                    dve.wait_ge(s_gain, 64)
                    for t in range(NT):
                        dve.wait_ge(s_gv, t + 1)
                        layer_norm(vln[:, t, :], gains[:, 0, :], gains[:, 1, :]).then_inc(s_vln, 1)
                if kind == "rv" and arg[0] == 0:
                    decay_strips()
                if kind == "split" and arg[0] == GV:
                    dve.wait_ge(s_whi, arg[1] + 1)
                    w_low(V, *arg).then_inc(s_gvlo, 1)
                if kind == "norm":
                    h = arg[0]
                    fence()
                    r = rstd(mv[:, :, 1], 2 * NT)
                    for g in (h - 1, h):
                        b_ = BANK["read", g][0]
                        for c in range(NT):
                            i = NT * (g % 2) + c
                            last = V.tensor_scalar(rnorm[:, g, c * P:(c + 1) * P], ps[:, b_, c * P:(c + 1) * P],
                                                   mv[:, i, 0:1], r[:, i:i + 1], ALU.subtract, ALU.mult)
                        last.then_inc(free[b_], 1)
                        fence().then_inc(s_norm, 1)
                if by != "dve" or kind == "outA":
                    continue
                dve.wait_ge(full[b], n + 1)
                bank = ps[:, b, :]
                bank4 = bank.rearrange("p (c n) -> p c n", c=4)
                if kind == "xT":
                    t, half = arg
                    ks = slice(4 * half, 4 * half + 4)
                    dve.wait_ge(s_xhi, 2 * t + half + 1)
                    V.tensor_tensor(xlo[:, t, ks, :], bank4, xhi[:, ks, t * P:(t + 1) * P].bitcast(f32),
                                    ALU.subtract).then_inc(free[b], 1)
                    fence().then_inc(s_xT, 1)
                elif kind == "keysT":
                    q = arg[0]
                    V.tensor_copy(keysT[:, 4 * q:4 * q + 4, :], bank4).then_inc(free[b], 1)
                    fence().then_inc(s_keysT, 1)
                elif kind == "mix":
                    h = arg[0]
                    bias = gains[:, 3, h * P:(h + 1) * P].unsqueeze(1).broadcast_to([P, NT, P])
                    t4 = tmp[:, h, :].rearrange("p (c n) -> p c n", c=NT)
                    V.tensor_tensor(t4, bank4, bias, ALU.add).then_inc(free[b], 1)
                    dve.wait_ge(s_gu, h + 1)
                    fence()
                    V.tensor_tensor(mixT[:, h, :], mixT[:, h, :], tmp[:, h, :], ALU.mult).then_inc(s_mix, 1)
                elif kind == "qk":
                    w, t = arg
                    if w == 0 and t == 0:
                        dve.wait_ge(s_rope, 16)
                    x1 = bank4[:, :, 0:64]
                    x2 = bank4[:, :, 64:128]
                    ct = cos[:, t, :].unsqueeze(1).broadcast_to([P, HEADS, 64])
                    sn = sin[:, t, :].unsqueeze(1).broadcast_to([P, HEADS, 64])
                    r4 = tmp[:, t % 2, :].rearrange("p (c n) -> p c n", c=HEADS)
                    if w or t >= 2:
                        dve.wait_ge(s_qkT, NT * w + t - 1)
                    a4 = tmp[:, 2, :].rearrange("p (c n) -> p c n", c=HEADS)
                    V.tensor_tensor(r4[:, :, 0:64], x1, ct, ALU.mult)
                    V.tensor_tensor(r4[:, :, 64:128], x2, ct, ALU.mult)
                    V.tensor_tensor(a4[:, :, 0:64], x2, sn, ALU.mult)
                    V.tensor_tensor(a4[:, :, 64:128], x1, sn, ALU.mult).then_inc(free[b], 1)
                    fence()
                    V.tensor_tensor(r4[:, :, 0:64], r4[:, :, 0:64], a4[:, :, 0:64], ALU.subtract)
                    V.tensor_tensor(r4[:, :, 64:128], r4[:, :, 64:128], a4[:, :, 64:128], ALU.add)
                    fence().then_inc(s_rot, 1)
                elif kind == "score":
                    h, m = arg
                    if m == 0:
                        dve.wait_ge(s_strip, h + 1)
                    c0 = SEQ - P - m * P
                    V.scalar_tensor_tensor(prob[h % 2][:, m, :], bank, SCALE, strip[:, h, c0:c0 + SEQ],
                                           ALU.mult, ALU.mult).then_inc(free[b], 1)
                    fence().then_inc(s_prob, 1)
                elif kind == "read":
                    h = arg[0]
                    first = NT * (h % 2)
                    for c in range(NT):
                        V.bn_stats(st[:, first + c, :], bank4[:, c, :])
                    fence()
                    for c in range(NT):
                        V.bn_aggr(mv[:, first + c, :], st[:, first + c, :])

            def residual(t, half):
                b, n = BANK["out", t, half]
                if half == 0:
                    dve.wait_ge(s_x[t], 32)
                dve.wait_ge(full[b], n + 1)
                z = xh[:, t * D + half * 512:t * D + half * 512 + 512]
                V.scalar_tensor_tensor(z, z, ALPHA, ps[:, b, :], ALU.mult, ALU.add).then_inc(free[b], 1)

            def first_norm(t, known=0):
                fence()
                layer_norm(xh[:, t * D:(t + 1) * D], lnp[:, 0, :], lnp[:, 1, :], s_h, known).then_inc(s_h, 1)

            def top16(src, values, index, spare):
                V.max(values[:, 0:8], src)
                fence()
                V.max_index(index[:, 0:8], values[:, 0:8], src)
                V.match_replace(spare, values[:, 0:8], src, NEG)
                fence()
                V.max(values[:, 8:16], spare)
                fence()
                V.max_index(index[:, 8:16], values[:, 8:16], spare)

            def choose(u, k, work=work1):
                eq = work[:, 0:512]
                cand = work[:, 0:256]
                sc = work[:, 512:1024].rearrange("p (a n) -> p a n", a=2)
                scores = sc[:, 0, :]
                if isinstance(u, int) and u < TILE0:
                    scores = S0[u]
                else:
                    V.tensor_copy(scores, S[:, bass.ts(u, 256)])
                    fence()
                for p in range(2):
                    top16(scores[:, p * NK:(p + 1) * NK], top[:, p, :], topi[:, p, :],
                          sc[:, 1, p * NK:(p + 1) * NK])
                fence()
                V.tensor_copy(topf[:], topi[:])
                a = top[:, 0, :].unsqueeze(2).broadcast_to([P, TOPK, TOPK])
                bb = top[:, 1, :].unsqueeze(1).broadcast_to([P, TOPK, TOPK])
                V.tensor_tensor(cand.rearrange("p (a b) -> p a b", a=TOPK), a, bb, ALU.add)
                fence()
                top16(cand, best[:, k, :], pos[:], sc[:, 0, :])
                fence()
                V.tensor_scalar(posab[:, 0, :], pos[:], 4, None, ALU.logical_shift_right)
                V.tensor_scalar(posab[:, 1, :], pos[:], 15, None, ALU.bitwise_and)
                V.tensor_scalar(negmax[:, k:k + 1], best[:, k, 0:1], -1.0, None, ALU.mult).then_inc(s_best, 1)
                fence()
                V.tensor_copy(posf[:], posab[:])
                fence()
                for p in range(2):
                    e3 = eq[:, p * 256:(p + 1) * 256].rearrange("p (k a) -> p k a", a=TOPK)
                    V.tensor_tensor(e3, posf[:, p, :].unsqueeze(2).broadcast_to([P, TOPK, TOPK]),
                                    iota16[:].unsqueeze(1).broadcast_to([P, TOPK, TOPK]), ALU.is_equal)
                fence()
                for p in range(2):
                    e3 = eq[:, p * 256:(p + 1) * 256].rearrange("p (k a) -> p k a", a=TOPK)
                    V.tensor_tensor(e3, e3, topf[:, p, :].unsqueeze(1).broadcast_to([P, TOPK, TOPK]), ALU.mult)
                fence()
                V.tensor_reduce(pick[:], eq.rearrange("p (q k a) -> p q k a", q=2, a=TOPK), AX.X, ALU.add)
                fence()
                V.scalar_tensor_tensor(idxu[:, k, :], pick[:, 0, :], float(NK), pick[:, 1, :],
                                       ALU.mult, ALU.add).then_inc(s_idxu, 1)
                fence()

            def add_unit(u, k, tile, n=TOPK):
                dve.wait_ge(s_vexp, 16 * u + n)
                yt = y[:, bass.ts(tile, D)]
                V.tensor_tensor(yt, yt, acc[k], ALU.add).then_inc(s_yadd, 1)

            def products(u, k, e0, e1, hcur=hcur1):
                for e in range(e0, e1):
                    dve.wait_ge(s_u[e % RING], 32 * u + 16 * (1 + e // RING))
                    V.tensor_tensor_reduce(out=urow[e % RING], in0=urow[e % RING], in1=hcur, scale=1.0,
                                           scalar=0.0, op0=ALU.mult, op1=ALU.add,
                                           accum_out=dots[:, k, e:e + 1]).then_inc(s_dot, 1)

            def publish(k):
                V.tensor_copy(idxv[:, k, :], idxu[:, k, :]).then_inc(s_idxv, 1)

            def weights(u, k):
                dve.wait_ge(s_exp, u + 1)
                V.reciprocal(rsum[:, k:k + 1], esum[:, k:k + 1])
                fence()
                dve.wait_ge(s_gel, u + 1)
                V.scalar_tensor_tensor(wgt[:, k, :], gel[:, k, :], rsum[:, k:k + 1], eg[:, k, :],
                                       ALU.mult, ALU.mult).then_inc(s_wgt, 1)

            def unit(u, k, tile, before, new_tile=False, scores=None):
                if new_tile:
                    V.tensor_copy(hcur1, xh[:, bass.ts(tile, D)])
                    fence()
                products(u, k, 0, TOPK // 2)
                if isinstance(u, int) and u == 2:
                    dve.wait_ge(s_y, 1)
                add_unit(u - 2, k, before)
                publish(k)
                if scores is not None:
                    dve.wait_ge(s_sc, scores)
                choose(u + 1, 1 - k)
                products(u, k, TOPK // 2, TOPK)
                weights(u, k)

            def finish_tile(tile):
                layer_norm(y[:, bass.ts(tile, D)], lnp[:, 0, :], lnp[:, 1, :], s_ln2).then_inc(s_ln2, 1)
                fence()

            dve.wait_ge(s_ln, 32)
            residual(0, 0)
            fence()
            V.bn_stats(st[:, 0, :], xh[:, 0:512])
            residual(0, 1)
            first_norm(0, known=1)
            fence()
            V.tensor_copy(hcur0, xh[:, 0:D])
            dve.wait_ge(s_sc0, 1)
            choose(0, 0, work0)
            publish(0)
            dve.wait_ge(s_sc0, 2)
            choose(1, 1, work0)
            products(0, 0, 0, 4, hcur0)
            residual(1, 0)
            residual(1, 1)
            residual(2, 0)
            products(0, 0, 4, 8, hcur0)
            residual(2, 1)
            products(0, 0, 8, 12, hcur0)
            products(0, 0, 12, TOPK, hcur0)
            weights(0, 0)
            residual(3, 0)
            first_norm(1)
            residual(3, 1)
            products(1, 1, 0, TOPK // 4, hcur0)
            first_norm(2)
            products(1, 1, TOPK // 4, TOPK // 2, hcur0)
            publish(1)
            dve.wait_ge(s_sc0, 3)
            choose(2, 0, work0)
            products(1, 1, TOPK // 2, TOPK, hcur0)
            weights(1, 1)
            first_norm(3)
            dve.wait_ge(s_wdone, 8)
            dve.wait_ge(s_sc0, TILE0)
            for u in range(2, PH):
                unit(u, u % 2, 0, 0, new_tile=u == 2, scores=2 * (u + 1 - TILE0) + 2 if u + 1 >= TILE0 else None)
            dve.wait_ge(s_y, NT)
            dve.wait_ge(s_const, 5)
            dve.wait_ge(s_ln, 64)
            with dve.Fori(1, NT) as tile:
                unit(tile * PH, 0, tile, before=tile - 1, new_tile=True, scores=2 * PH)
                unit(tile * PH + 1, 1, tile, before=tile - 1)
                finish_tile(tile - 1)
                with dve.Fori(1, PH // 2) as j:
                    unit(tile * PH + 2 * j, 0, tile, before=tile)
                    unit(tile * PH + 2 * j + 1, 1, tile, before=tile)
            add_unit(UNITS - 2, 0, NT - 1)
            fence()
            for e in range(LAST, TOPK):
                if e == TOPK - 1:
                    add_unit(UNITS - 1, 1, NT - 1, LAST)
                    fence()
                dve.wait_ge(s_v[e % RING], 32 * (UNITS - 1) + 16 * (1 + e // RING))
                V.scalar_tensor_tensor(y[:, (NT - 1) * D:], vrow[e % RING], wgt[:, 1, e:e + 1],
                                       y[:, (NT - 1) * D:], ALU.mult, ALU.add)
                fence()
            finish_tile(NT - 1)

        @block.tensor
        def _(pe):
            T = nc.tensor

            def product(dst, lhs, rhs, n):
                for i in range(n):
                    last = T.matmul(dst, lhs(i), rhs(i), start=(i == 0), stop=(i == n - 1))
                return last

            def project(dst, g, first, x_of, w_of, x_left=True):
                xs, ws = (lambda k: x_of(xhi4, k), lambda k: x_of(xlo, k)), (w_hi(g), w_lo(g))
                for n, (xp, wp) in enumerate(((0, 0), (1, 0), (0, 1))):
                    for k in range(KC):
                        if first and k % (KC // WPART) == 0 and n != 1:
                            c = k * WPART // KC
                            if n == 0:
                                pe.wait_ge(s_whi, WPART * g + c + 1)
                            elif g == GV:
                                pe.wait_ge(s_gvlo, c + 1)
                            else:
                                pe.wait_ge(s_wlo, WPART * (g - 1) + c + 1)
                        a, b_ = xs[xp](k), w_of(ws[wp], k)
                        last = T.matmul(dst, *((a, b_) if x_left else (b_, a)),
                                        start=(n == 0 and k == 0), stop=(n == 2 and k == KC - 1))
                return last

            def project_tokens(dst, g, t):
                return project(dst, g, t == 0, lambda x_, k: x_[:, t, k, :], lambda w_, k: w_[:, k, :])

            def group(half):
                pe.wait_ge(s_wo[half], 16)
                return wring[:, 2 + half, :, :]

            xhi4 = xhi.rearrange("p k (t n) -> p t k n", t=NT)

            def add_rows(u, k, e0=0, e1=TOPK, end=TOPK):
                fixed = isinstance(u, int)
                ring = vrow0 if fixed and u == 0 else vrow
                if e0 == 0 and not (fixed and u < 2):
                    pe.wait_ge(s_yadd, u - 1)
                for e in range(e0, e1):
                    pe.wait_ge(s_v[e % RING], 32 * u + 16 * (1 + e // RING))
                    pe.wait_ge(s_diag, 16 * u + e + 1)
                    for half in range(2):
                        last = T.matmul(acc[k][:, half * 512:(half + 1) * 512], diag[:, e % NDIAG, :],
                                        ring[e % RING][:, half * 512:(half + 1) * 512],
                                        start=(e == 0), stop=(e == end - 1))
                    last.then_inc(s_vexp, 1)

            pe.wait_ge(s_const, 4)
            for kind, arg, by, b, n in JOBS:
                if kind in ("split", "norm"):
                    continue
                if kind == "V":
                    if arg[0:2] == (0, 0):
                        for b in range(4):
                            pe.wait_ge(free[b], USED[b])
                    add_rows(arg[0], arg[0] % 2, arg[1], arg[2])
                    continue
                if n and not (kind == "out" and arg[0] < 2):
                    pe.wait_ge(free[b], n)
                bank = ps[:, b, :]
                bank4 = bank.rearrange("p (c n) -> p c n", c=4)
                used = None
                if kind == "xT":
                    t, half = arg
                    if half == 0:
                        pe.wait_ge(s_x[t], 16)
                    for i in range(4):
                        k = 4 * half + i
                        last = T.transpose(bank4[:, i, :], xh[:, t * D + k * P:t * D + (k + 1) * P], ident[:])
                elif kind == "gv":
                    t = arg[0]
                    pe.wait_ge(s_xT, 2 * t + 2)
                    last = project_tokens(bank, GV, t)
                    used = t == NT - 1
                elif kind == "wsT":
                    pe.wait_ge(s_ws, 16)
                    for h in range(HEADS):
                        last = T.transpose(bank4[:, h, :], ws_raw[:, h, :], ident[:])
                elif kind == "keysT":
                    if arg[0] == 0:
                        pe.wait_ge(s_keys, 16)
                    for i in range(4):
                        last = T.transpose(bank4[:, i, :], keys_raw[:, 4 * arg[0] + i, :], ident[:])
                elif kind == "gu":
                    c = arg[0]
                    last = project(bank, GU, c == 0, lambda x_, k: x_[:, :, k, :],
                                   lambda w_, k: w_[:, k, c * P:(c + 1) * P], x_left=False)
                    used = c == 3
                elif kind == "mix":
                    h = arg[0]
                    if h == 0:
                        pe.wait_ge(s_vln, NT)
                        pe.wait_ge(s_wsT, 1)
                    for c in range(NT):
                        last = T.matmul(bank4[:, c, :], vln[:, c, h * P:(h + 1) * P], wsT[:, h, :],
                                        start=True, stop=True)
                elif kind == "qk":
                    w_, t = arg
                    last = project_tokens(bank, GQ + w_, t)
                    used = t == NT - 1
                elif kind == "qkT":
                    w_, t = arg
                    pe.wait_ge(s_rot, NT * w_ + t + 1)
                    for h in range(HEADS):
                        last = T.transpose(bank4[:, h, :], tmp[:, t % 2, h * P:(h + 1) * P], ident[:])
                elif kind in ("rv", "rg"):
                    t = arg[0]
                    last = project_tokens(bank, GRV if kind == "rv" else GG, t)
                    used = t == NT - 1
                elif kind == "score":
                    h, m = arg
                    if h == 0 and m == 0:
                        pe.wait_ge(s_qkT, 2 * NT)
                    last = T.matmul(bank, qkT[:, 1, h, m * P:(m + 1) * P], qkT[:, 0, h, :], start=True, stop=True)
                elif kind == "read":
                    h = arg[0]
                    if h == 0:
                        pe.wait_ge(s_rv, NT)
                    pe.wait_ge(s_prob, NT * (h + 1))
                    for c in range(NT):
                        last = product(bank4[:, c, :], lambda m: prob[h % 2][:, m, c * P:(c + 1) * P],
                                       lambda m: rv[:, m, h * P:(h + 1) * P], NT)
                elif kind == "rT":
                    h = arg[0]
                    pe.wait_ge(s_rn, h + 1)
                    for c in range(NT):
                        last = T.transpose(bank4[:, c, :], rnorm[:, h, c * P:(c + 1) * P], ident[:])
                elif kind == "outA":
                    t, half = arg
                    pe.wait_ge(s_mix, HEADS)
                    w = group(half)
                    for k in range(4):
                        T.matmul(bank, mixT[:, k, t * P:(t + 1) * P], w[:, k, :], start=(k == 0), stop=False)
                    continue
                elif kind == "out" and arg[0] < 2:
                    t, half = arg
                    pe.wait_ge(s_rT, HEADS)
                    w = group(half)
                    for k in range(4, KC):
                        last = T.matmul(bank, mixT[:, k, t * P:(t + 1) * P], w[:, k, :], start=False,
                                        stop=(k == KC - 1))
                elif kind == "out":
                    t, half = arg
                    w = group(half)
                    last = product(bank, lambda k: mixT[:, k, t * P:(t + 1) * P], lambda k: w[:, k, :], KC)
                elif kind == "hT":
                    t, half = arg
                    pe.wait_ge(s_h, 2 * t + half + 1)
                    for i in range(4):
                        k = 4 * half + i
                        last = T.transpose(bank4[:, i, :], xh[:, t * D + k * P:t * D + (k + 1) * P], ident[:])
                elif kind == "query0":
                    h = arg[0]
                    pe.wait_ge(s_wq[h % 2], 16 * (h // 2 + 1))
                    for p in range(2):
                        for k in range(KC):
                            if h == 0 and p == 0 and k % 4 == 0:
                                pe.wait_ge(s_hT, k // 4 + 1)
                            last = T.matmul(bank4[:, p, :], wq[:, h % 2, k, p * P:(p + 1) * P], xT[:, k, 0:P],
                                            start=(k == 0), stop=(k == KC - 1))
                elif kind == "keys0":
                    h = arg[0]
                    pe.wait_ge(s_qh0, h + 1)
                    if h == 0:
                        pe.wait_ge(s_keysT, 4)
                    for p in range(2):
                        last = T.matmul(bank4[:, p, :], qh0[:, h % 2, p, :], keysT[:, 2 * h + p, :],
                                        start=True, stop=True)
                elif kind == "query":
                    i_, p = arg
                    n_ = TILE0 + i_
                    t0 = 0 if HEAD_ORDER[i_] >= TILE0 else 1
                    if p == 0:
                        pe.wait_ge(s_wq[n_ % 2], 16 * (n_ // 2 + 1))
                        if i_ == 0:
                            pe.wait_ge(s_hT, 2 * NT)
                    last = product(bank[:, t0 * P:], lambda k: wq[:, n_ % 2, k, p * P:(p + 1) * P],
                                   lambda k: xT[:, k, t0 * P:], KC)
                elif kind == "keys":
                    i_, p = arg
                    h = HEAD_ORDER[i_]
                    pe.wait_ge(s_qh, 2 * i_ + p + 1)
                    for t in range(0 if h >= TILE0 else 1, NT):
                        last = T.matmul(bank4[:, t, :], qh[:, i_ % 2, p, t * P:(t + 1) * P],
                                        keysT[:, 2 * h + p, :], start=True, stop=True)
                last.then_inc(full[b], 1)
                if kind == "query0" or (kind == "query" and arg[1] == 1):
                    T.drain().then_inc(s_wqd, 1)
                if used:
                    T.drain().then_inc(s_wdone, 1)
                if kind == "out" and arg == (NT - 1, 1):
                    T.drain().then_inc(s_wdone, 2)
                if kind == "score" and arg == (HEADS - 1, NT - 1):
                    T.drain().then_inc(s_scored, 1)

            for u in range(EARLY, PH):
                add_rows(u, u % 2)
            with pe.Fori(PH // 2, UNITS // 2 - 1) as pair:
                add_rows(2 * pair, 0)
                add_rows(2 * pair + 1, 1)
            add_rows(UNITS - 2, 0)
            add_rows(UNITS - 1, 1, 0, LAST, end=LAST)


_INS = ["x", "w_in", "sgu_ln_w", "sgu_ln_b", "sgu_w_s", "sgu_b", "ret_decay_fwd", "ret_decay_bwd", "ret_gn_w",
        "w_out", "ln1_w", "ln1_b", "peer_w_q", "peer_sub_keys", "peer_u", "peer_v", "ln2_w", "ln2_b"]


def kernel(**inputs):
    import numpy as _np
    import concourse.bacc as _bacc
    from concourse import mybir as _mybir
    from concourse.bass_utils import run_bass_kernel_spmd as _run

    nc = _bacc.Bacc("TRN2", target_bir_lowering=False, num_devices=1)
    arrays, args = {}, []
    for name in _INS:
        a = _np.ascontiguousarray(inputs[name])
        arrays[f"in_{name}_dram"] = a
        args.append(nc.dram_tensor(f"in_{name}_dram", a.shape, _mybir.dt.from_np(a.dtype), kind="ExternalInput").ap())
    half = P // 2
    inv = _np.float32(10000.0) ** (-_np.arange(half, dtype=_np.float32) / _np.float32(half))
    ang = _np.arange(SEQ, dtype=_np.float32)[:, None] * inv[None, :].astype(_np.float32)
    table = _np.stack([_np.cos(ang), _np.sin(ang)], axis=1).astype(_np.float32)
    table = _np.ascontiguousarray(table.reshape(NT, P, 2, half).transpose(1, 0, 2, 3))
    arrays["rope_dram"] = table
    args.append(nc.dram_tensor("rope_dram", table.shape, _mybir.dt.float32, kind="ExternalInput").ap())
    out = nc.dram_tensor("out_dram", (1, SEQ, D), _mybir.dt.float32, kind="ExternalOutput").ap()
    layer(nc, *args, out)
    r = _run(nc, [arrays], core_ids=[0])
    return r.results[0]["out_dram"]
```
